# Optimizing a Trainium2 kernel written in Bass

```python
import jax, jax.numpy as jnp
from jax import lax
import numpy as np

D_MODEL = 1024
BATCH = 1
SEQ = 512
DEPTH = 2
DEC_BATCH = 1
DEC_SEQ = 32
PAST_LEN = 1024

CHUNK = 64
POOL_WINDOWS = (2, 4, 8, 16)
POOL_GROUPS = len(POOL_WINDOWS)
POOL_WIDTH = D_MODEL // 2
POOL_GD = POOL_WIDTH // POOL_GROUPS
POOL_BUF = max(POOL_WINDOWS) - 1
RET_HEADS = 4
RET_DK = D_MODEL // 8
RET_DV = D_MODEL // 8
RET_WIDTH = RET_HEADS * RET_DV
N_BRANCH = 2
IN_WIDTH = POOL_WIDTH + 4 * RET_WIDTH + N_BRANCH * D_MODEL
D_FF = ((8 * D_MODEL // 3 + 127) // 128) * 128
N_MOD = 9
ROPE_BASE = 10000.0
EPS = 1e-6

kernel_name = "hybrid_pool_retention_streaming_step"

F32 = jnp.float32

def rmsnorm(x, g):
    xf = x.astype(F32)
    r = lax.rsqrt(jnp.mean(xf * xf, axis=-1, keepdims=True) + EPS)
    return (xf * r).astype(x.dtype) * g

def swiglu(h, w_up, w_down):
    a, b = jnp.split(h @ w_up, 2, axis=-1)
    return (jax.nn.silu(a) * b) @ w_down

def rope(x, pos):
    half = x.shape[-1] // 2
    inv = ROPE_BASE ** (-jnp.arange(half, dtype=F32) / half)
    ang = pos.astype(F32)[:, None] * inv[None, :]
    cos = jnp.cos(ang)[None, :, None, :]
    sin = jnp.sin(ang)[None, :, None, :]
    x1 = x[..., :half].astype(F32)
    x2 = x[..., half:].astype(F32)
    return jnp.concatenate([x1 * cos - x2 * sin, x2 * cos + x1 * sin], axis=-1).astype(x.dtype)

def log_gammas():
    return jnp.log1p(-jnp.exp2(-5.0 - jnp.arange(RET_HEADS, dtype=F32)))

def pool_mix(u, buf, start, pool_map, pool_scale):
    B, T, P = u.shape
    L = POOL_BUF
    full = jnp.concatenate([buf.astype(u.dtype), u], axis=1)
    cs0 = jnp.pad(jnp.cumsum(full.astype(F32), axis=1), ((0, 0), (1, 0), (0, 0)))
    pos = start + jnp.arange(T)
    ys = []
    for gi, w in enumerate(POOL_WINDOWS):
        sl = slice(gi * POOL_GD, (gi + 1) * POOL_GD)
        s = cs0[:, L + 1:L + 1 + T, sl] - cs0[:, L + 1 - w:L + 1 - w + T, sl]
        cnt = jnp.minimum(w, pos + 1).astype(F32)
        ys.append((s / cnt[None, :, None]).astype(u.dtype) - u[..., sl])
    y = jnp.stack(ys, axis=2)
    y = jnp.einsum("btgc,gcd->btgd", y, pool_map).reshape(B, T, P) * pool_scale
    return y, full[:, -L:]

def retention(q, k, v, state):
    B, T, H, dk = q.shape
    dv = v.shape[-1]
    blk = min(CHUNK, T)
    n = T // blk
    lg = log_gammas()
    i = jnp.arange(blk, dtype=F32)
    diff = i[:, None] - i[None, :]
    dmask = jnp.where(diff[None] >= 0, jnp.exp(lg[:, None, None] * jnp.maximum(diff, 0.0)[None]), 0.0)
    xi = jnp.exp(lg[None, :] * (i[:, None] + 1.0))
    zeta = jnp.exp(lg[None, :] * (blk - 1.0 - i[:, None]))
    g_blk = jnp.exp(lg * blk)

    def to_chunks(a):
        return a.astype(F32).reshape(B, n, blk, H, a.shape[-1]).transpose(1, 0, 2, 3, 4)

    def step(S, inp):
        qc, kc, vc = inp
        sc = jnp.einsum("bihd,bjhd->bhij", qc, kc) * dmask[None]
        inner = jnp.einsum("bhij,bjhe->bihe", sc, vc)
        cross = jnp.einsum("bihd,bhde->bihe", qc, S) * xi[None, :, :, None]
        S = g_blk[None, :, None, None] * S + jnp.einsum("bjhd,bjhe->bhde", kc * zeta[None, :, :, None], vc)
        return S, inner + cross

    S, ys = lax.scan(step, state.astype(F32), (to_chunks(q), to_chunks(k), to_chunks(v)))
    y = ys.transpose(1, 0, 2, 3, 4).reshape(B, T, H, dv)
    return y, S

def layer(x, c, start, pool_buf, ret_state, w_ada, b_ada, norm_g, w_up1, w_down1, w_up2, w_down2,
          w_in, pool_map, pool_scale, w_pool_out, ret_gn, w_ret_out, w_o):
    B, T, D = x.shape
    mod = (jax.nn.silu(c) @ w_ada + b_ada).reshape(B, N_MOD, 1, D)
    h = rmsnorm(x, norm_g[0]) * (1 + mod[:, 1]) + mod[:, 0]
    x = x + 0.5 * mod[:, 2] * swiglu(h, w_up1, w_down1)
    h = rmsnorm(x, norm_g[1]) * (1 + mod[:, 4]) + mod[:, 3]
    z = h @ w_in
    cuts = np.cumsum([POOL_WIDTH, RET_WIDTH, RET_WIDTH, RET_WIDTH, RET_WIDTH]).tolist()
    z_pool, z_q, z_k, z_v, z_g, z_gate = jnp.split(z, cuts, axis=-1)
    pool_y, new_buf = pool_mix(z_pool, pool_buf, start, pool_map, pool_scale)
    pos = start + jnp.arange(T)
    q = rope(z_q.reshape(B, T, RET_HEADS, RET_DK), pos)
    k = rope(z_k.reshape(B, T, RET_HEADS, RET_DK), pos) * (RET_DK ** -0.5)
    v = z_v.reshape(B, T, RET_HEADS, RET_DV)
    y, new_state = retention(q, k, v, ret_state)
    mu = jnp.mean(y, axis=-1, keepdims=True)
    var = jnp.mean(jnp.square(y - mu), axis=-1, keepdims=True)
    yn = ((y - mu) * lax.rsqrt(var + EPS)).reshape(B, T, RET_WIDTH).astype(x.dtype) * ret_gn
    ret_y = jax.nn.silu(z_g) * yn
    gates = jax.nn.sigmoid(z_gate.astype(F32)).astype(x.dtype).reshape(B, T, N_BRANCH, D)
    merged = gates[:, :, 0] * (pool_y @ w_pool_out) + gates[:, :, 1] * (ret_y @ w_ret_out)
    x = x + mod[:, 5] * (merged @ w_o)
    h = rmsnorm(x, norm_g[2]) * (1 + mod[:, 7]) + mod[:, 6]
    x = x + 0.5 * mod[:, 8] * swiglu(h, w_up2, w_down2)
    return x, new_buf, new_state.astype(ret_state.dtype)

def trunk(x, c, start, pool_bufs, ret_states, w_ada, b_ada, norm_g, w_up1, w_down1, w_up2, w_down2,
          w_in, pool_map, pool_scale, w_pool_out, ret_gn, w_ret_out, w_o, final_g):
    bufs, states = [], []
    for l in range(DEPTH):
        x, nb, ns = layer(x, c, start, pool_bufs[l], ret_states[l], w_ada[l], b_ada[l], norm_g[l],
                          w_up1[l], w_down1[l], w_up2[l], w_down2[l], w_in[l], pool_map[l],
                          pool_scale[l], w_pool_out[l], ret_gn[l], w_ret_out[l], w_o[l])
        bufs.append(nb)
        states.append(ns)
    return rmsnorm(x, final_g), jnp.stack(bufs, axis=0), jnp.stack(states, axis=0)

def setup_inputs(seed: int = 0) -> dict:
    key = jax.random.key(seed)
    ks = jax.random.split(key, 24)
    D = D_MODEL

    def nrm(k, shape, s):
        return jax.random.normal(k, shape, jnp.float32) * s

    return {
        "x_prompt": nrm(ks[0], (BATCH, SEQ, D), 1.0),
        "x_sample": nrm(ks[1], (DEC_BATCH, DEC_SEQ, D), 1.0),
        "c_prompt": nrm(ks[2], (BATCH, D), 1.0),
        "c_sample": nrm(ks[3], (DEC_BATCH, D), 1.0),
        "cache_pool": nrm(ks[4], (DEPTH, DEC_BATCH, POOL_BUF, POOL_WIDTH), 1.0),
        "state_ret": nrm(ks[5], (DEPTH, DEC_BATCH, RET_HEADS, RET_DK, RET_DV), 0.3),
        "w_ada": nrm(ks[6], (DEPTH, D, N_MOD * D), 0.5 * D ** -0.5),
        "b_ada": nrm(ks[7], (DEPTH, N_MOD * D), 0.01),
        "norm_g": 1.0 + nrm(ks[8], (DEPTH, 3, D), 0.1),
        "w_up1": nrm(ks[9], (DEPTH, D, 2 * D_FF), D ** -0.5),
        "w_down1": nrm(ks[10], (DEPTH, D_FF, D), D_FF ** -0.5),
        "w_up2": nrm(ks[11], (DEPTH, D, 2 * D_FF), D ** -0.5),
        "w_down2": nrm(ks[12], (DEPTH, D_FF, D), D_FF ** -0.5),
        "w_in": nrm(ks[13], (DEPTH, D, IN_WIDTH), D ** -0.5),
        "pool_map": nrm(ks[14], (DEPTH, POOL_GROUPS, POOL_GD, POOL_GD), POOL_GD ** -0.5),
        "pool_scale": 1.0 + nrm(ks[15], (DEPTH, POOL_WIDTH), 0.1),
        "w_pool_out": nrm(ks[16], (DEPTH, POOL_WIDTH, D), POOL_WIDTH ** -0.5),
        "ret_gn": 1.0 + nrm(ks[17], (DEPTH, RET_WIDTH), 0.1),
        "w_ret_out": nrm(ks[18], (DEPTH, RET_WIDTH, D), RET_WIDTH ** -0.5),
        "w_o": nrm(ks[19], (DEPTH, D, D), D ** -0.5),
        "final_g": 1.0 + nrm(ks[20], (D,), 0.1),
    }

def reference(x_prompt, x_sample, c_prompt, c_sample, cache_pool, state_ret, w_ada, b_ada, norm_g,
              w_up1, w_down1, w_up2, w_down2, w_in, pool_map, pool_scale, w_pool_out, ret_gn,
              w_ret_out, w_o, final_g):
    zero_bufs = jnp.zeros((DEPTH, x_prompt.shape[0], POOL_BUF, POOL_WIDTH), x_prompt.dtype)
    zero_states = jnp.zeros((DEPTH, x_prompt.shape[0], RET_HEADS, RET_DK, RET_DV), F32)
    y_prompt, pool_prompt, ret_prompt = trunk(
        x_prompt, c_prompt, 0, zero_bufs, zero_states, w_ada, b_ada, norm_g, w_up1, w_down1,
        w_up2, w_down2, w_in, pool_map, pool_scale, w_pool_out, ret_gn, w_ret_out, w_o, final_g)
    y_sample, pool_sample, ret_sample = trunk(
        x_sample, c_sample, PAST_LEN, cache_pool, state_ret, w_ada, b_ada, norm_g, w_up1, w_down1,
        w_up2, w_down2, w_in, pool_map, pool_scale, w_pool_out, ret_gn, w_ret_out, w_o, final_g)
    return (y_prompt, y_sample, pool_prompt, ret_prompt, pool_sample, ret_sample)


_drawn_inputs = setup_inputs


def setup_inputs(seed=0):
    import zlib

    import numpy as np

    out = dict(_drawn_inputs(seed))
    spreads = {}
    factors = {'ret_gn': 3.525}
    for name, (base, spread) in spreads.items():
        noise = np.random.default_rng([zlib.crc32(name.encode()), seed]).standard_normal(out[name].shape)
        drawn = base * np.exp(spread * noise) if base else spread * noise
        out[name] = __import__('jax').numpy.asarray(drawn.astype(out[name].dtype))
    for name, factor in factors.items():
        out[name] = (out[name] * factor).astype(out[name].dtype)
    return out
```

```python
from contextlib import ExitStack

import numpy as np

import concourse.bass as bass
from concourse import mybir

ALU = mybir.AluOpType
ACT = mybir.ActivationFunctionType
F32 = mybir.dt.float32
F32R = mybir.dt.float32r

P = 128
D = 1024
TP, TS = 512, 32
T = TP + TS
HT = T // 2
KD = D // P
DEPTH = 2
FF = 2816
HK = FF // P // 2
HEADS, DK = 4, 128
GROUPS, HALO = 4, 15
WINDOWS = (2, 4, 8, 16)
PW = HALO + TP + HALO + TS
S0 = HALO + TP + HALO
SLOT = 2 * KD * P
EPS = 1e-6
N_MOD = 9
SETS = 3
CHUNKS = 6
JB = TP // P
TOK = JB + 1

C_POOL, C_Q, C_K, C_V, C_G, C_GATE = (512 * n for n in range(6))
PARTS = ((0, 0, HT, 0, 0), (1, 0, TP - HT, HT, 0), (1, TP - HT, HT, TP, 1))
SPANS = ((0, TP), (TP, T))

R_B, R_N, R_PS, R_GN, R_FG, R_ALL = 0, 72, 96, 100, 104, 112
R_CACHE = HALO * GROUPS

K_ID, K_ONE, K_COS, K_SIN, K_MASK = 0, 128, 256, 256 + T, 256 + 2 * T
K_XI = K_MASK + HEADS * TP
K_ZETA = K_XI + HEADS * TS
K_ZETAS = K_ZETA + HEADS * JB
K_GBLK = K_ZETAS + HEADS
K_INV = K_GBLK + HEADS
K_EPS = K_INV + GROUPS * 16
K_ALL = K_EPS + 1

UNITS = 124
PAIR = 2 * 30 + 47
STEPS = 267
MID = (("qk", 0), ("qk", 1), ("qk", 2), ("qk", 3), ("v", 0), ("v", 1), ("head", 0), ("split", 0),
       ("pool", 0), ("mean", 0), ("head", 1), ("var", 0), ("split", 1), ("pool", 1), ("mean", 1),
       ("head", 2), ("var", 1), ("split", 2), ("map", 0), ("mean", 2), ("head", 3), ("var", 2),
       ("split", 3), ("map", 1), ("mean", 3), ("var", 3), ("g", 0), ("g", 1))


class Tally:

    def __init__(self, each, start=0):
        self.each, self.start, self.n, self.layer, self.inner = each, start, 0, 0, 0

    def at(self, more=0):
        return self.layer * self.each + (self.inner + (self.start + self.n + more))

    def step(self, k=1):
        self.n += k


class Layers:

    def __init__(self, eng, tallies, passed):
        self.eng, self.tallies, self.passed = eng, tallies, passed

    def fence(self):
        self.eng.sem_inc(self.passed, 1)

    def layers(self, body):
        self.fence()
        with self.eng.Fori(0, DEPTH) as layer:
            for t in self.tallies:
                t.start, t.n, t.layer = t.start + t.n, 0, layer
            body(layer)
            for t in self.tallies:
                assert t.n == t.each, (t.name, t.n, t.each)
        for t in self.tallies:
            t.start, t.n, t.layer = t.start + DEPTH * t.each, 0, 0

    def repeat(self, count, body, **adds):
        before = {t: t.n for t in self.tallies}
        self.fence()
        with self.eng.Fori(0, count) as i:
            for t in self.tallies:
                t.inner = i * adds[t.name] if adds.get(t.name) else 0
            body(i)
            for t in self.tallies:
                assert t.n - before[t] == adds.get(t.name, 0), (t.name, t.n - before[t])
        for t in self.tallies:
            t.inner, t.n = 0, before[t] + count * adds.get(t.name, 0)


def halves(ap):
    return ap.rearrange("p (h t) -> p h t", h=2)


def trunk_kernel(nc, x_prompt, x_sample, c_prompt, c_sample, cache_pool, state_ret, w_ada, b_ada,
                 norm_g, w_up1, w_down1, w_up2, w_down2, w_in, pool_map, pool_scale, w_pool_out,
                 ret_gn, w_ret_out, w_o, final_g, consts,
                 y_prompt, y_sample, pool_prompt, ret_prompt, pool_sample, ret_sample):
    ctx = ExitStack()
    with ctx:
        def sb(name, shape, dt=F32, stack=ctx):
            return stack.enter_context(nc.sbuf_tensor(name, [P, *shape], dt))

        def sem(name):
            return ctx.enter_context(nc.semaphore(name))

        x = sb("x", [KD, T])
        h_hi, h_lo = sb("h_hi", [KD, T], F32R), sb("h_lo", [KD, T], F32R)
        raw = [sb(f"raw{p}", [SLOT]) for p in range(2)]
        w_hi = [sb(f"w_hi{p}", [SLOT], F32R) for p in range(2)]
        w_lo = [sb(f"w_lo{p}", [SLOT], F32R) for p in range(2)]
        const = sb("const", [K_ALL])
        ones = sb("ones", [P], F32R)
        vec_t = sb("vec_t", [DEPTH * R_ALL])
        cache_t = sb("cache_t", [DEPTH * R_CACHE])
        c_silu = sb("c_silu", [2 * KD])
        c_parts = sb("c_parts", [KD, 4], F32R)
        mod_t = sb("mod_t", [24, 4])
        mod_s = sb("mod_s", [24, 2])
        coef = sb("coef", [SETS, 3, KD, 2])
        s_old = sb("s_old", [HEADS, DK])
        s_new = [sb(f"s_new{p}", [2, DK]) for p in range(2)]
        tmp = sb("tmp", [2, T])
        rstd = sb("rstd", [T])
        acted = sb("acted", [2, 2, HT])
        prod = sb("prod", [2, 2, HT])

        with ExitStack() as st:
            rows_in = sb("rows_in", [DEPTH, 2, P], stack=st)
            x_in = sb("x_in", [TOK, D], stack=st)
            y_out = sb("y_out", [2, D], stack=st)
        with ExitStack() as st:
            u_hi, u_lo = sb("u_hi", [HK, T], F32R, st), sb("u_lo", [HK, T], F32R, st)
            mod_row = sb("mod_row", [CHUNKS, 512], stack=st)
            ada_raw = sb("ada_raw", [2, 512], stack=st)
            ada_hi, ada_lo = sb("ada_hi", [2, 512], F32R, st), sb("ada_lo", [2, 512], F32R, st)
        with ExitStack() as st:
            q = sb("q", [HEADS, T], stack=st)
            with ExitStack() as st2:
                k = sb("k", [HEADS, T], stack=st2)
                v = sb("v", [TOK, HEADS * DK], stack=st2)
                yp_hi, yp_lo = sb("yp_hi", [GROUPS, T], F32R, st2), sb("yp_lo", [GROUPS, T], F32R, st2)
                with ExitStack() as st3:
                    masked = sb("masked", [2, TP], stack=st3)
                    kz = sb("kz", [TOK, DK], stack=st3)
                    pf = sb("pf", [2, PW], stack=st3)
                    win = [sb(f"win{n}", [PW], stack=st3) for n in range(2)]
                    first = sb("first", [16], stack=st3)
                    gn_hi, gn_lo = sb("gn_hi", [T], F32R, st3), sb("gn_lo", [T], F32R, st3)
                    masked_s = sb("masked_s", [TS], stack=st3)
                    q_xi = sb("q_xi", [TS], stack=st3)
                    pool_rows = sb("pool_rows", [2, 512], stack=st3)
                m_hi, m_lo = sb("m_hi", [KD // 2, T], F32R, st2), sb("m_lo", [KD // 2, T], F32R, st2)
            ry_hi, ry_lo = sb("ry_hi", [HEADS, T], F32R, st), sb("ry_lo", [HEADS, T], F32R, st)

        acc = ctx.enter_context(nc.psum_tensor("acc", [P, 4, 512], F32))
        ps_mod = ctx.enter_context(nc.psum_tensor("ps_mod", [P, 512], F32))
        ps_misc = ctx.enter_context(nc.psum_tensor("ps_misc", [P, 512], F32))
        ps_sum = ctx.enter_context(nc.psum_tensor("ps_sum", [P, 2, 512], F32))

        ident = const[:, K_ID:K_ID + P]
        cos, sin = const[:, K_COS:K_COS + T], const[:, K_SIN:K_SIN + T]
        eps = const[:, K_EPS:K_EPS + 1]

        passed = sem("passed")
        const_in = sem("const_in")
        rows_landed = sem("rows_landed")
        raw_landed = [sem(f"raw_landed{p}") for p in range(2)]
        w_rounded = sem("w_rounded")
        w_split = sem("w_split")
        ada_landed = sem("ada_landed")
        ada_rounded = sem("ada_rounded")
        ada_split = sem("ada_split")
        ada_used = sem("ada_used")
        acc_ready = [sem(f"acc_ready{p}") for p in range(2)]
        acc_free = [sem(f"acc_free{p}") for p in range(2)]
        rows_t = sem("rows_t")
        rows_copied = sem("rows_copied")
        c_ok = sem("c_ok")
        mod_sum = sem("mod_sum")
        mod_copied = sem("mod_copied")
        mod_turned = sem("mod_turned")
        mod_cols = sem("mod_cols")
        acted_ok = sem("acted_ok")
        u_ready = sem("u_ready")
        x_squared = sem("x_squared")
        sq_split = sem("sq_split")
        sums_ready = sem("sums_ready")
        root_ok = sem("root_ok")
        scaled = sem("scaled")
        h_rounded = sem("h_rounded")
        h_ready = sem("h_ready")
        swapped = sem("swapped")
        halo_ready = sem("halo_ready")
        tails_t = sem("tails_t")
        tails_ok = sem("tails_ok")
        tails_out = sem("tails_out")
        yp_ready = sem("yp_ready")
        sc_ready = sem("sc_ready")
        masked_ok = sem("masked_ok")
        y_ready = sem("y_ready")
        y_copied = sem("y_copied")
        s_landed = sem("s_landed")
        s_out = [sem(f"s_out{p}") for p in range(2)]
        gn_split = sem("gn_split")
        gn_squared = sem("gn_squared")
        side_ready = sem("side_ready")
        out_copied = sem("out_copied")
        out_done = [sem(f"out_done{p}") for p in range(2)]
        dve_step = sem("dve_step")

        def pair_banks(p, columns=HT):
            return acc[:, 2 * p:2 * p + 2, 0:columns]

        block = ctx.enter_context(nc.Block())

        def tallies(**each):
            made = []
            for name, (n, start) in each.items():
                t = Tally(n, start)
                t.name = name
                made.append(t)
            return made

        @block.sync
        def _(sp):
            unit, = made = tallies(unit=(UNITS, 0))
            loops = Layers(sp, made, passed)

            sp.dma_start(const[:, :], consts).then_inc(const_in, 16)
            for n, t in enumerate((c_prompt, c_sample)):
                sp.dma_start(rows_in[R_CACHE + n * KD:R_CACHE + (n + 1) * KD, 0, 1, :],
                             t.rearrange("a (k f) -> (a k) f", f=P)).then_inc(rows_landed, 16)
            for layer in range(DEPTH):
                for r0, r1, t in ((R_B, R_N, b_ada[layer:layer + 1, :].rearrange("a (k f) -> (a k) f", f=P)),
                                  (R_N, R_PS, norm_g[layer, :, :].rearrange("a (k f) -> (a k) f", f=P)),
                                  (R_PS, R_GN, pool_scale[layer:layer + 1, :].rearrange("a (k f) -> (a k) f", f=P)),
                                  (R_GN, R_FG, ret_gn[layer:layer + 1, :].rearrange("a (k f) -> (a k) f", f=P)),
                                  (R_FG, R_ALL, final_g.rearrange("(k f) -> k f", f=P))):
                    sp.dma_start(rows_in[r0:r1, layer, 0, :], t).then_inc(rows_landed, 16)
                sp.dma_start(rows_in[0:R_CACHE, layer, 1, :],
                             cache_pool[layer, 0].rearrange("t (g f) -> (t g) f", f=P)).then_inc(rows_landed, 16)
            sp.dma_start(x_in[:, 0:JB, :], x_prompt[0].rearrange("(b p) f -> p b f", p=P)).then_inc(rows_landed, 16)
            sp.dma_start(x_in[0:TS, JB, :], x_sample[0]).then_inc(rows_landed, 16)

            def load(p, first_part, second_part):
                sp.wait_ge(w_split, unit.at(1))
                loops.fence()
                for dst, src in (first_part, second_part):
                    sp.dma_start(dst, src).then_inc(raw_landed[p], 16)
                unit.step()

            def rows_of(w, layer):
                return w.rearrange("l (k p) n -> p l k n", p=P)[:, layer]

            def blocks(p, w, layer, c0, c1):
                to = raw[p][:, :].rearrange("p (b k n) -> p b k n", b=2, k=KD)
                load(p, (to[:, 0], rows_of(w, layer)[:, :, bass.ds(c0, P)]),
                     (to[:, 1], rows_of(w, layer)[:, :, bass.ds(c1, P)]))

            def rows(p, w, layer, k0, nk, c0, nc_):
                to = raw[p][:, 0:nk * nc_].rearrange("p (k n) -> p k n", k=nk)
                a = nk // 2
                load(p, (to[:, 0:a], rows_of(w, layer)[:, k0:k0 + a, bass.ds(c0, nc_)]),
                     (to[:, a:nk], rows_of(w, layer)[:, k0 + a:k0 + nk, bass.ds(c0, nc_)]))

            def ffn(layer, w_up, w_down):
                for half in range(2):
                    j0 = half * HK
                    q0 = half

                    def up(i, p, j):
                        blocks(p, w_up, layer, j * P, j * P + FF)

                    def two_up(i):
                        for e in range(2):
                            up(i, (q0 + e) % 2, i * 2 + (j0 + e))
                    loops.repeat(HK // 2, two_up, unit=2)
                    up(0, q0, j0 + HK - 1)

                    def two_down(i):
                        for e in range(2):
                            rows((q0 + 1 + e) % 2, w_down, layer, j0, HK, i * (2 * P) + e * P, P)
                    loops.repeat(KD // 2, two_down, unit=2)

            def layer_loads(layer):
                def ada(i):
                    for kh in range(2):
                        rows(kh, w_ada, layer, kh * 4, 4, i * 512, 512)
                loops.repeat(CHUNKS, ada, unit=2)
                ffn(layer, w_up1, w_down1)
                sp.dma_start(s_old[:, :, :], state_ret.rearrange("l a h p n -> p l (a h) n")[:, layer])\
                    .then_inc(s_landed, 16)
                for kind, n in MID:
                    if kind == "qk":
                        blocks(n % 2, w_in, layer, C_Q + n * P, C_K + n * P)
                    elif kind == "v":
                        rows(n, w_in, layer, 0, KD, C_V + n * 256, 256)
                    elif kind == "pool":
                        blocks(n, w_in, layer, C_POOL + n * 256, C_POOL + n * 256 + P)
                    elif kind == "map":
                        to = raw[n][:, 0:2 * P].rearrange("p (g n) -> p g n", g=2)
                        src = pool_map.rearrange("l g p n -> p l g n")[:, layer]
                        load(n, (to[:, 0:1], src[:, 2 * n:2 * n + 1]), (to[:, 1:2], src[:, 2 * n + 1:2 * n + 2]))
                    elif kind == "g":
                        blocks(n, w_in, layer, C_G + n * 256, C_G + n * 256 + P)
                for mh in range(2):
                    def gate_out(i):
                        n = i * P + mh * 512
                        blocks(0, w_in, layer, C_GATE + n, C_GATE + D + n)
                        to = raw[1][:, 0:2 * 4 * P].rearrange("p (b k n) -> p b k n", b=2, k=4)
                        load(1, (to[:, 0], rows_of(w_pool_out, layer)[:, :, bass.ds(n, P)]),
                             (to[:, 1], rows_of(w_ret_out, layer)[:, :, bass.ds(n, P)]))
                    loops.repeat(4, gate_out, unit=2)

                    def outs(i):
                        for e in range(2):
                            rows(e, w_o, layer, 4 * mh, 4, i * 512 + e * 256, 256)
                    loops.repeat(2, outs, unit=2)
                ffn(layer, w_up2, w_down2)
            loops.layers(layer_loads)

            for t in range(TOK):
                sp.wait_ge(out_copied, t + 1)
                if t < JB:
                    sp.dma_start(y_prompt[0, t * P:(t + 1) * P, :], y_out[:, t % 2, :]).then_inc(out_done[t % 2], 16)
                else:
                    sp.dma_start(y_sample[0], y_out[0:TS, t % 2, :]).then_inc(out_done[t % 2], 16)
            sp.wait_ge(out_done[0], 16 * 3)
            sp.wait_ge(out_done[1], 16 * 2)

        @block.gpsimd
        def _(pool):
            with pool.Fori(0, DEPTH) as layer:
                pool.wait_ge(h_ready, layer * (SETS * KD) + KD)
                pool.sem_inc(passed, 1)
                with pool.Fori(0, 2 * CHUNKS) as c:
                    for kk in range(4):
                        pool.wait_ge(ada_split, layer * (8 * CHUNKS) + (c * 4 + (kk + 1)))
                        pool.dma_start(ada_raw[:, :, :], w_ada.rearrange("l (k p) n -> p l k n", p=P)
                                       [:, layer, 2 * kk:2 * kk + 2, bass.ds(c * 512 + CHUNKS * 512, 512)])\
                            .then_inc(ada_landed, 16)

        @block.tensor
        def _(pe):
            unit, ada, pair0, pair1, chunk, squares, hs, u_t, tails, yp_t, mask_t, y_t, gn_t, side_t, layers = \
                made = tallies(unit=(UNITS, 0), ada=(48, 0), pair0=(PAIR, 0), pair1=(PAIR, 0), chunk=(18, 0),
                               squares=(24, 0), h=(24, 0), u=(88, 0), tails=(2, 0), yp=(4, 0), mask=(24, 0),
                               y=(4, 0), gn=(8, 0), side=(24, 0), layers=(1, 0))
            pairs = (pair0, pair1)
            loops = Layers(pe, made, passed)

            mm = pe.matmul

            def begin_unit():
                pe.wait_ge(w_split, unit.at(1 + 2))
                unit.step()

            def take(p):
                pe.wait_ge(acc_free[p], pairs[p].at(1))

            def done(p, ins):
                ins.then_inc(acc_ready[p], 1)
                pairs[p].step()

            def product(out, ws, xs, nk):
                for kk in range(nk):
                    for n, (a, b) in enumerate(((0, 0), (0, 1), (1, 0))):
                        last = mm(out, ws(a, kk), xs(b, kk), start=(kk == 0 and n == 0),
                                  stop=(kk == nk - 1 and n == 2))
                return last

            def cols(hf):
                return slice(hf * HT, (hf + 1) * HT)

            def parts(hi, lo, hf):
                return lambda b, kk: (hi, lo)[b][:, kk, cols(hf)]

            def w_view(p, pattern, n, **sizes):
                return [t[p][:, 0:n].rearrange(pattern, **sizes) for t in (w_hi, w_lo)]

            def block_unit(p, between=None):
                begin_unit()
                w = w_view(p, "p (b k n) -> p b k n", SLOT, b=2, k=KD)
                for hf in range(2):
                    take(hf)
                    for b in range(2):
                        last = product(acc[:, 2 * hf + b, 0:HT], lambda a, kk: w[a][:, b, kk, :],
                                       parts(h_hi, h_lo, hf), KD)
                    done(hf, last)
                    if between:
                        between(hf)

            def ada_mm(kk, hi, lo, bank=ps_mod):
                for n, w in enumerate((hi, lo)):
                    last = mm(bank[0:4, :], c_parts[:, kk, :], w, start=(kk == 0 and n == 0),
                              stop=(kk == KD - 1 and n == 1))
                return last

            def ada_small(kp):
                if kp == 0:
                    pe.wait_ge(mod_copied, chunk.at(2))
                pe.wait_ge(ada_split, ada.at(1 + 1))
                for e in range(2):
                    last = ada_mm(2 * kp + e, ada_hi[:, e, :], ada_lo[:, e, :])
                ada.step()
                if kp == 3:
                    last.then_inc(mod_sum, 1)
                    chunk.step()
                else:
                    last.then_inc(ada_used, 1)

            def turn_mods():
                pe.wait_ge(mod_copied, chunk.at(2))
                loops.fence()
                for j in range(24):
                    last = pe.matmul(ps_misc[:, 4 * j:4 * j + 4], mod_row[0:4, j // 4, (j % 4) * P:(j % 4 + 1) * P],
                                     ident[0:4, 0:4], is_transpose=True, start=True, stop=True)
                last.then_inc(mod_turned, 1)

            def column_sums(nk):
                for kk in range(nk):
                    pe.wait_ge(sq_split, squares.at(1 + 2))
                    squares.step()
                    for hf in range(2):
                        for b, part in enumerate((h_hi, h_lo)):
                            last = mm(ps_sum[:, hf, 0:HT], ones[:, :], part[:, kk, cols(hf)],
                                      start=(kk == 0 and b == 0), stop=(kk == nk - 1 and b == 1))
                last.then_inc(sums_ready, 1)

            def wait_h():
                hs.step(KD)
                pe.wait_ge(h_ready, hs.at())

            pe.wait_ge(const_in, 16)
            pe.wait_ge(rows_landed, 16 * (2 + 6 * DEPTH + 2))
            for layer in range(DEPTH):
                pe.matmul(ps_misc[:, layer * 192:layer * 192 + R_ALL], rows_in[0:R_ALL, layer, 0, :],
                          ident[0:R_ALL, 0:R_ALL], is_transpose=True, start=True, stop=True)
                n = R_CACHE + (2 * KD if layer == 0 else 0)
                last = pe.matmul(ps_misc[:, layer * 192 + R_ALL:layer * 192 + R_ALL + n], rows_in[0:n, layer, 1, :],
                                 ident[0:n, 0:n], is_transpose=True, start=True, stop=True)
            last.then_inc(rows_t, 1)
            for kk in range(KD):
                p = kk % 2
                take(p)
                for b in range(JB):
                    pe.matmul(acc[:, 2 * p, b * P:(b + 1) * P], x_in[:, b, kk * P:(kk + 1) * P], ident,
                              is_transpose=True, start=True, stop=True)
                done(p, pe.matmul(acc[:, 2 * p + 1, 0:TS], x_in[0:TS, JB, kk * P:(kk + 1) * P], ident[0:TS, 0:TS],
                                  is_transpose=True, start=True, stop=True))

            def ffn(with_ada):
                for half in range(2):
                    q0 = half

                    def two_up(i):
                        for e in range(2):
                            block_unit((q0 + e) % 2, (lambda hf: ada_small(2 * e + hf)) if with_ada else None)
                    n = 2 if with_ada else 0
                    loops.repeat(HK // 2, two_up, unit=2, pair0=2, pair1=2, ada=2 * n, chunk=n // 2)

                    def two_small(hf):
                        ada_small(2 * hf)
                        ada_small(2 * hf + 1)
                    block_unit(q0, two_small if with_ada else None)
                    u_t.step(2 * HK)
                    pe.wait_ge(u_ready, u_t.at())

                    def two_down(i):
                        for e in range(2):
                            slot = (q0 + 1 + e) % 2
                            begin_unit()
                            w = w_view(slot, "p (k n) -> p k n", HK * P, k=HK)
                            take(e)
                            for hf in range(2):
                                last = product(acc[:, 2 * e + hf, 0:HT], lambda a, kk: w[a][:, kk, :],
                                               parts(u_hi, u_lo, hf), HK)
                            done(e, last)
                    loops.repeat(KD // 2, two_down, unit=2, pair0=1, pair1=1)
                    if with_ada:
                        turn_mods()

            def head(hd):
                own = slice(hd * DK, (hd + 1) * DK)
                take(0)
                for b in range(JB):
                    pe.matmul(acc[:, 0, b * P:(b + 1) * P], k[:, hd, b * P:(b + 1) * P], ident,
                              is_transpose=True, start=True, stop=True)
                done(0, pe.matmul(acc[0:TS, 1, 0:P], k[:, hd, TP:T], ident, is_transpose=True, start=True, stop=True))

                bank = (ps_mod, ps_misc)

                def scores(b):
                    pe.matmul(bank[b % 2][:, 0:TP - b * P], k[:, hd, b * P:(b + 1) * P], q[:, hd, b * P:TP],
                              start=True, stop=True).then_inc(sc_ready, 1)

                def values(b):
                    mask_t.step()
                    pe.wait_ge(masked_ok, mask_t.at())
                    pe.matmul(ps_sum[:, 0, b * P:TP], v[:, b, own], masked[:, b % 2, 0:TP - b * P],
                              start=(b == 0), stop=(b == JB - 1))

                if hd == 0:
                    pe.wait_ge(acc_free[1], pair1.at(1))
                    layers.step()
                    pe.wait_ge(s_landed, layers.at() * 16)
                scores(0)
                if hd == 1 or hd == 2:
                    tails.step()
                    pe.wait_ge(tails_ok, tails.at())
                scores(1)
                pe.wait_ge(y_copied, y_t.at(1))
                values(0)
                scores(2)
                values(1)
                scores(3)
                values(2)
                pe.matmul(ps_sum[0:TS, 1, 0:TS], k[:, hd, TP:T], q[:, hd, TP:T], start=True, stop=True)\
                    .then_inc(sc_ready, 1)
                values(3)
                mask_t.step(2)
                pe.wait_ge(masked_ok, mask_t.at())
                pe.matmul(ps_sum[:, 1, 64:64 + TS], v[0:TS, JB, own], masked_s[0:TS, :], start=True, stop=False)
                pe.matmul(ps_sum[:, 1, 64:64 + TS], s_old[:, hd, :], q_xi[:, :], start=False, stop=True)\
                    .then_inc(y_ready, 1)
                y_t.step()
                pe.wait_ge(acc_free[0], pair0.at(1))
                take(1)
                for b in range(JB):
                    pe.matmul(acc[:, 2, 0:DK], kz[:, b, :], v[:, b, own], start=(b == 0), stop=(b == JB - 1))
                done(1, pe.matmul(acc[:, 3, 0:DK], kz[0:TS, JB, :], v[0:TS, JB, own], start=True, stop=True))

            def group_sum(p):
                gn_t.step()
                pe.wait_ge(gn_split, gn_t.at())
                take(p)
                for hf in range(2):
                    for b, part in enumerate((gn_hi, gn_lo)):
                        last = pe.matmul(acc[:, 2 * p + hf, 0:HT], ones[:, :], part[:, cols(hf)],
                                         start=(b == 0), stop=(b == 1))
                done(p, last)

            def middle():
                for kind, n in MID:
                    if kind in ("qk", "g"):
                        block_unit(n % 2)
                    elif kind == "pool":
                        block_unit(n)
                        pe.wait_ge(acc_free[1], pair1.at(1))
                        for s, c0 in enumerate((HALO + TP - HALO, PW - HALO)):
                            for b in range(2):
                                last = pe.matmul(ps_misc[0:HALO, (2 * s + b) * P:(2 * s + b + 1) * P],
                                                 pf[:, b, c0:c0 + HALO], ident, is_transpose=True, start=True, stop=True)
                        last.then_inc(tails_t, 1)
                    elif kind == "v":
                        begin_unit()
                        w = w_view(n, "p (k n) -> p k n", SLOT, k=KD)
                        for t in range(TOK):
                            p = (n * TOK + t) % 2
                            rows = P if t < JB else TS
                            take(p)
                            done(p, product(acc[0:rows, 2 * p, 0:256],
                                            lambda a, kk: (h_hi, h_lo)[a][:, kk, t * P:t * P + rows],
                                            lambda b, kk: w[b][:, kk, :], KD))
                    elif kind == "map":
                        begin_unit()
                        w = w_view(n, "p (g n) -> p g n", 2 * P, g=2)
                        for e in range(2):
                            g = 2 * n + e
                            yp_t.step()
                            pe.wait_ge(yp_ready, yp_t.at())
                            take(e)
                            for hf in range(2):
                                last = product(acc[:, 2 * e + hf, 0:HT], lambda a, kk: w[a][:, e, :],
                                               lambda b, kk: (yp_hi, yp_lo)[b][:, g, cols(hf)], 1)
                            done(e, last)
                    elif kind == "head":
                        head(n)
                    elif kind in ("mean", "var"):
                        group_sum(kind == "var")
                side_t.step(4 + 4)
                pe.wait_ge(side_ready, side_t.at())
                for mh in range(2):
                    def gate_out(i):
                        block_unit(0)
                        begin_unit()
                        w = w_view(1, "p (b k n) -> p b k n", 2 * 4 * P, b=2, k=4)
                        for hf in range(2):
                            take(hf)
                            product(acc[:, 2 * hf, 0:HT], lambda a, kk: w[a][:, 0, kk, :], parts(yp_hi, yp_lo, hf), 4)
                            done(hf, product(acc[:, 2 * hf + 1, 0:HT], lambda a, kk: w[a][:, 1, kk, :],
                                             parts(ry_hi, ry_lo, hf), 4))
                    loops.repeat(4, gate_out, unit=2, pair0=2, pair1=2)
                    side_t.step(8)
                    pe.wait_ge(side_ready, side_t.at())

                    def outs(i):
                        for e in range(2):
                            begin_unit()
                            w = w_view(e, "p (k n) -> p k n", 4 * 256, k=4)
                            for b in range(2):
                                take(b)
                                for hf in range(2):
                                    last = product(acc[:, 2 * b + hf, 0:HT],
                                                   lambda a, kk: w[a][:, kk, b * P:(b + 1) * P],
                                                   parts(m_hi, m_lo, hf), 4)
                                done(b, last)
                    loops.repeat(2, outs, unit=2, pair0=2, pair1=2)

            def one_layer(layer):
                column_sums(KD)

                def ada_big(bank):
                    for kh in range(2):
                        begin_unit()
                        w = w_view(kh, "p (k n) -> p k n", SLOT, k=4)
                        if kh == 0:
                            pe.wait_ge(mod_copied, chunk.at(1))
                        for kk in range(4):
                            last = ada_mm(kh * 4 + kk, w[0][:, kk, :], w[1][:, kk, :], bank)
                        last.then_inc(mod_sum, 1)
                    chunk.step()
                loops.repeat(CHUNKS // 2, lambda i: [ada_big(b) for b in (ps_mod, ps_misc)], unit=4, chunk=2)
                turn_mods()
                wait_h()
                ffn(True)
                column_sums(KD)
                wait_h()
                middle()
                column_sums(KD)
                wait_h()
                ffn(False)
            pe.wait_ge(rows_copied, 5)
            loops.layers(one_layer)

            column_sums(KD)
            wait_h()
            for t in range(TOK):
                p, rows = t % 2, (P if t < JB else TS)
                if t < 2:
                    take(p)
                else:
                    pe.wait_ge(out_copied, t - 1)
                for kk in range(KD):
                    last = pe.matmul(acc[0:rows, 2 * p + kk // 4, (kk % 4) * P:(kk % 4 + 1) * P],
                                     x[:, kk, t * P:t * P + rows], ident, is_transpose=True, start=True, stop=True)
                done(p, last)

        @block.scalar
        def _(act):
            land0, land1, ada, used, pair0, pair1, chunk, sets, norms, squares, scale_t, pf_t, y_t, side_t = \
                made = tallies(land0=(UNITS // 2, 0), land1=(UNITS // 2, 0), ada=(48, 0),
                               used=(36, 0), pair0=(PAIR, 0), pair1=(PAIR, 0), chunk=(24, 0), sets=(3, 0),
                               norms=(3, 0), squares=(24, 0), scale=(24, 0), pf=(2, 0), y=(4, 0), side=(24, 0))
            pairs, lands = (pair0, pair1), (land0, land1)
            loops = Layers(act, made, passed)

            act.sem_inc(mod_copied, 2)
            act.sem_inc(y_copied, 1)
            act.sem_inc(tails_out, 32)
            for p in range(2):
                act.sem_inc(s_out[p], 32)
            for p in range(2):
                act.sem_inc(acc_free[p], 1)

            def split(p):
                act.wait_ge(raw_landed[p], lands[p].at(1) * 32)
                act.activation(w_hi[p][:, :], raw[p][:, :], ACT.Copy).then_inc(w_rounded, 1)
                lands[p].step()

            def ada_high():
                act.wait_ge(ada_landed, ada.at(1) * 16)
                act.activation(ada_hi[:, :, :], ada_raw[:, :, :], ACT.Copy).then_inc(ada_rounded, 1)
                ada.step()

            def copy_row(row, bank=ps_mod):
                chunk.step()
                act.wait_ge(mod_sum, chunk.at())
                act.activation(mod_row[0:4, row, :], bank[0:4, :], ACT.Copy).then_inc(mod_copied, 1)

            def wait_group(p):
                act.wait_ge(acc_ready[p], pairs[p].at(1))
                pairs[p].step()

            def copy_mods():
                sets.step()
                act.wait_ge(mod_turned, sets.at())
                act.activation(mod_t[:, :, :].rearrange("p a b -> p (a b)"), ps_misc[:, 0:96], ACT.Copy)\
                    .then_inc(mod_cols, 1)

            def square(n, par, x_new):
                act.wait_ge(*x_new)
                act.wait_ge(sq_split, squares.at(1))
                act.activation(tmp[:, par, :], x[:, n, :], ACT.Square).then_inc(x_squared, 1)
                squares.step()

            def norm_root():
                norms.step()
                act.wait_ge(sums_ready, norms.at())
                act.activation(halves(rstd[:, :]), ps_sum[:, :, 0:HT], ACT.Sqrt, scale=1.0 / D, bias=eps)\
                    .then_inc(root_ok, 1)

            def round_h(s):
                for kk in range(KD):
                    scale_t.step()
                    act.wait_ge(scaled, scale_t.at())
                    for g, (a, b) in enumerate(SPANS):
                        last = act.activation(h_hi[:, kk, a:b], tmp[:, kk % 2, a:b], ACT.Identity,
                                              bias=coef[:, s, 0, kk, g:g + 1], scale=1.0)
                    last.then_inc(h_rounded, 1)

            act.wait_ge(rows_t, 1)
            for layer in range(DEPTH):
                o = layer * 192
                act.activation(vec_t[:, layer * R_ALL:(layer + 1) * R_ALL], ps_misc[:, o:o + R_ALL], ACT.Copy)\
                    .then_inc(rows_copied, 1)
                act.activation(cache_t[:, layer * R_CACHE:(layer + 1) * R_CACHE],
                               ps_misc[:, o + R_ALL:o + R_ALL + R_CACHE], ACT.Copy).then_inc(rows_copied, 1)
            act.activation(c_silu[:, :], ps_misc[:, R_ALL + R_CACHE:R_ALL + R_CACHE + 2 * KD], ACT.Silu)\
                .then_inc(c_ok, 1)
            for kk in range(KD):
                p = kk % 2
                wait_group(p)
                act.activation(x[:, kk, 0:TP], acc[:, 2 * p, :], ACT.Copy)
                act.activation(x[:, kk, TP:T], acc[:, 2 * p + 1, 0:TS], ACT.Copy).then_inc(acc_free[p], 1)
                square(kk, kk % 2, (acc_free[p], pairs[p].at(1)))

            def down_steps(n, p, last_half):
                wait_group(p)
                if last_half:
                    square(n, p, (acc_free[p], pairs[p].at(1)))

            def ffn(with_ada, last_stage):
                if with_ada:
                    ada_high()
                for half in range(2):
                    q0 = half

                    def run(slot, smalls, row, last=False):
                        for hf in range(2):
                            wait_group(hf)
                            act.activation(acted[:, hf, 0, :], acc[:, 2 * hf, 0:HT], ACT.Silu).then_inc(acted_ok, 1)
                            for kp in smalls[hf]:
                                if kp == 3:
                                    copy_row(row)
                                else:
                                    used.step()
                                    act.wait_ge(ada_used, used.at())
                                if not (half and last and kp == 3):
                                    ada_high()
                        split(slot)

                    def two_up(i):
                        for e in range(2):
                            smalls = ((2 * e,), (2 * e + 1,)) if with_ada else ((), ())
                            run((q0 + e) % 2, smalls, i)
                    n = 4 if with_ada else 0
                    loops.repeat(HK // 2, two_up, land0=1, land1=1, pair0=2, pair1=2, ada=n,
                                 used=3 * n // 4, chunk=n // 4)
                    run(q0, ((0, 1), (2, 3)) if with_ada else ((), ()), CHUNKS - 1, True)

                    def down(n, e, more=True):
                        down_steps(n, e, half == 1)
                        if more:
                            split((q0 + 1 + e) % 2)
                    end = half == 1 and last_stage
                    turns = KD // 2 - (1 if end else 0)
                    loops.repeat(turns, lambda i: [down(i * 2 + e, e) for e in range(2)], land0=1, land1=1,
                                 pair0=1, pair1=1, squares=2 * half)
                    if end:
                        for e in range(2):
                            down(KD - 2 + e, e, more=False)
                    if with_ada:
                        copy_mods()

            def middle():
                def head(hd):
                    wait_group(0)
                    for b in range(JB):
                        act.activation(kz[:, b, :], acc[:, 0, b * P:(b + 1) * P], ACT.Copy,
                                       scale=const[:, K_ZETA + hd * JB + b:K_ZETA + hd * JB + b + 1])
                    act.activation(kz[0:TS, JB, :], acc[0:TS, 1, 0:P], ACT.Copy,
                                   scale=const[0:TS, K_ZETAS + hd:K_ZETAS + hd + 1]).then_inc(acc_free[0], 1)
                    y_t.step()
                    act.wait_ge(y_ready, y_t.at())
                    act.activation(q[:, hd, 0:TP], ps_sum[:, 0, :], ACT.Copy)
                    act.activation(q[:, hd, TP:T], ps_sum[:, 1, 64:64 + TS], ACT.Copy).then_inc(y_copied, 1)
                    pairs[1].step()
                    act.wait_ge(acc_free[1], pair1.at(1))
                    act.dma_start(ret_prompt.rearrange("l a h p n -> p l (a h) n")[:, loops.layer, hd, :],
                                  s_new[hd % 2][:, 0, :]).then_inc(s_out[hd % 2], 16)
                    act.dma_start(ret_sample.rearrange("l a h p n -> p l (a h) n")[:, loops.layer, hd, :],
                                  s_new[hd % 2][:, 1, :]).then_inc(s_out[hd % 2], 16)

                for kind, n in MID:
                    if kind == "qk":
                        for hf in range(2):
                            wait_group(hf)
                            z = tmp[:, hf, :].rearrange("p (a t) -> p a t", a=2)
                            act.activation(z[64:128], acc[0:64, 2 * hf:2 * hf + 2, 0:HT], ACT.Copy)
                            act.activation(z[0:64], acc[64:128, 2 * hf:2 * hf + 2, 0:HT], ACT.Copy)\
                                .then_inc(swapped, 1)
                        split(n % 2)
                    elif kind == "v":
                        for t in range(TOK):
                            p, rows = (n * TOK + t) % 2, (P if t < JB else TS)
                            wait_group(p)
                            act.activation(v[0:rows, t, n * 256:(n + 1) * 256], acc[0:rows, 2 * p, 0:256], ACT.Copy)\
                                .then_inc(acc_free[p], 1)
                        split(n)
                    elif kind == "pool":
                        pf_t.step()
                        act.wait_ge(halo_ready, pf_t.at())
                        for hf in range(2):
                            wait_group(hf)
                            if hf == 0:
                                act.activation(pf[:, :, HALO:HALO + HT], pair_banks(0), ACT.Copy)\
                                    .then_inc(acc_free[0], 1)
                            else:
                                act.activation(pf[:, :, HALO + HT:HALO + TP], acc[:, 2:4, 0:TP - HT], ACT.Copy)
                                act.activation(pf[:, :, S0:PW], acc[:, 2:4, TP - HT:HT], ACT.Copy)\
                                    .then_inc(acc_free[1], 1)
                        split(n)
                        act.wait_ge(tails_t, pf_t.at())
                        for s in range(2):
                            last = act.activation(pool_rows[0:HALO, s, n * 256:(n + 1) * 256],
                                                  ps_misc[0:HALO, s * 256:(s + 1) * 256], ACT.Copy)
                        last.then_inc(tails_ok, 1)
                        if n == 1:
                            act.wait_ge(tails_ok, pf_t.at())
                            for s, out in enumerate((pool_prompt, pool_sample)):
                                act.dma_start(out.rearrange("l a t f -> t l (a f)")[:, loops.layer, :],
                                              pool_rows[0:HALO, s, :]).then_inc(tails_out, 16)
                    elif kind == "map":
                        for e in range(2):
                            wait_group(e)
                        side_t.step(2)
                        split(n)
                    elif kind == "head":
                        head(n)
                    elif kind == "mean":
                        pairs[0].step()
                        act.wait_ge(acc_free[0], pair0.at(1))
                        act.activation(tmp[:, 0, :], q[:, n, :], ACT.Square).then_inc(gn_squared, 1)
                    elif kind == "var":
                        wait_group(1)
                        act.activation(halves(rstd[:, :]), pair_banks(1), ACT.Sqrt, scale=1.0 / DK, bias=eps)\
                            .then_inc(acc_free[1], 1)
                    elif kind == "g":
                        for hf in range(2):
                            wait_group(hf)
                            if n:
                                side_t.step()
                                act.wait_ge(side_ready, side_t.at())
                            act.activation(acted[:, hf, :, :], pair_banks(hf), ACT.Silu).then_inc(acc_free[hf], 1)
                        split(n)

                for mh in range(2):
                    def gate_out(i):
                        for hf in range(2):
                            wait_group(hf)
                            act.activation(acted[:, hf, :, :], pair_banks(hf), ACT.Tanh, scale=0.5)\
                                .then_inc(acc_free[hf], 1)
                        split(0)
                        for hf in range(2):
                            wait_group(hf)
                        split(1)
                    loops.repeat(4, gate_out, land0=1, land1=1, pair0=2, pair1=2)

                    def outs(i):
                        for e in range(2):
                            for b in range(2):
                                down_steps(i * 4 + (2 * e + b), b, mh == 1)
                            split(e)
                    loops.repeat(2, outs, land0=1, land1=1, pair0=2, pair1=2, squares=4 * mh)

            def one_layer(layer):
                loops.layer = layer
                split(0)
                split(1)
                norm_root()

                def ada_rows(i):
                    for e, bank in enumerate((ps_mod, ps_misc)):
                        chunk.step()
                        act.wait_ge(mod_sum, chunk.at())
                        split(0)
                        copy_row(i * 2 + e, bank)
                        split(1)
                loops.repeat(CHUNKS // 2, ada_rows, land0=2, land1=2, chunk=4)
                copy_mods()
                round_h(0)
                ffn(True, False)
                norm_root()
                round_h(1)
                middle()
                norm_root()
                round_h(2)
                ffn(False, True)
                side_t.step(24 - 6)
                act.wait_ge(tails_out, layer * 32 + 64)
            loops.layers(one_layer)

            norm_root()
            for t in range(TOK):
                p, rows = t % 2, (P if t < JB else TS)
                wait_group(p)
                if t >= 2:
                    act.wait_ge(out_done[p], 16 * (t // 2))
                act.activation(y_out[0:rows, p, :].rearrange("p (b n) -> p b n", b=2), acc[0:rows, 2 * p:2 * p + 2, :],
                               ACT.Copy).then_inc(out_copied, 1)
            act.wait_ge(tails_out, 32 * DEPTH + 32)
            for p in range(2):
                act.wait_ge(s_out[p], 64 * DEPTH + 32)

        @block.vector
        def _(dve):
            unit, ada, pair0, pair1, sets, norms, squares, h_t, u_t, swap_t, tails, mask_t, sc_t, y_t, gn_t, sq_t, \
                steps, layers = made = tallies(
                    unit=(UNITS, 0), ada=(48, 0), pair0=(PAIR, 0), pair1=(PAIR, 0), sets=(3, 0), norms=(3, 0),
                    squares=(24, 0), h=(24, 0), u=(88, 0), swap=(8, 0), tails=(2, 0), mask=(24, 0), sc=(20, 0),
                    y=(4, 0), gn=(8, 0), sq=(4, 0), steps=(STEPS, 0), layers=(1, 0))
            pairs = (pair0, pair1)
            loops = Layers(dve, made, passed)

            dve.sem_inc(w_split, 2)
            dve.sem_inc(ada_split, 1)
            dve.sem_inc(sq_split, 2)

            def step(ins):
                ins.then_inc(dve_step, 1)
                steps.step()

            def settled():
                dve.wait_ge(dve_step, steps.at())

            def f(ap):
                return ap.bitcast(F32)

            def cols(hf):
                return slice(hf * HT, (hf + 1) * HT)

            def two_parts(hi, lo, src, done):
                step(dve.tensor_copy(hi, src))
                settled()
                dve.tensor_tensor(lo, src, f(hi), ALU.subtract).then_inc(done, 1)

            def freed(p):
                dve.wait_ge(acc_free[p], pairs[p].at(1))

            def split(p):
                dve.wait_ge(w_rounded, unit.at(1))
                dve.tensor_tensor(w_lo[p][:, :], raw[p][:, :], f(w_hi[p][:, :]), ALU.subtract).then_inc(w_split, 1)
                unit.step()

            def ada_low():
                dve.wait_ge(ada_rounded, ada.at(1))
                dve.tensor_tensor(ada_lo[:, :, :], ada_raw[:, :, :], f(ada_hi[:, :, :]), ALU.subtract)\
                    .then_inc(ada_split, 1)
                ada.step()

            def square_parts(n, par):
                squares.step()
                dve.wait_ge(x_squared, squares.at())
                two_parts(h_hi[:, n, :], h_lo[:, n, :], tmp[:, par, :], sq_split)

            def coefficients(s, layer):
                sets.step()
                dve.wait_ge(mod_cols, sets.at())
                for g in range(2):
                    step(dve.scalar_tensor_tensor(mod_s[:, :, g], mod_t[:, :, g], 1.0, mod_t[:, :, 2 + g],
                                                  ALU.mult, ALU.add))
                settled()
                o = layer * R_ALL
                for g in range(2):
                    step(dve.tensor_tensor(mod_s[:, :, g], mod_s[:, :, g], vec_t[:, bass.ds(o + (R_B + 24 * s), 24)],
                                           ALU.add))
                settled()
                step(dve.tensor_copy(coef[:, s, 0, :, :], mod_s[:, 0:KD, :]))
                for g in range(2):
                    step(dve.scalar_tensor_tensor(coef[:, s, 1, :, g], mod_s[:, KD:2 * KD, g], 1.0,
                                                  vec_t[:, bass.ds(o + (R_N + KD * s), KD)], ALU.add, ALU.mult))
                step(dve.tensor_scalar(coef[:, s, 2, :, :], mod_s[:, 2 * KD:, :], 0.5, None, ALU.mult))
                settled()

            def reciprocal_root():
                norms.step()
                dve.wait_ge(root_ok, norms.at())
                step(dve.reciprocal(rstd[:, :], rstd[:, :]))
                settled()

            def make_h(s):
                def scale(kk):
                    for g, (a, b) in enumerate(SPANS):
                        last = dve.scalar_tensor_tensor(tmp[:, kk % 2, a:b], x[:, kk, a:b], coef[:, s, 1, kk, g:g + 1],
                                                        rstd[:, a:b], ALU.mult, ALU.mult)
                    last.then_inc(scaled, 1)
                scale(0)
                for kk in range(KD):
                    if kk + 1 < KD:
                        if kk:
                            dve.wait_ge(h_ready, h_t.at())
                        scale(kk + 1)
                    h_t.step()
                    dve.wait_ge(h_rounded, h_t.at())
                    for g, (a, b) in enumerate(SPANS):
                        last = dve.scalar_tensor_tensor(h_lo[:, kk, a:b], tmp[:, kk % 2, a:b],
                                                        coef[:, s, 0, kk, g:g + 1], f(h_hi[:, kk, a:b]),
                                                        ALU.add, ALU.subtract)
                    last.then_inc(h_ready, 1)

            def update_x(n, p, s):
                dve.wait_ge(acc_ready[p], pairs[p].at(1))
                pairs[p].step()
                for hf, a, b, c, g in PARTS:
                    last = dve.scalar_tensor_tensor(x[:, n, c:c + b - a], acc[:, 2 * p + hf, a:b],
                                                    coef[:, s, 2, n, g:g + 1], x[:, n, c:c + b - a],
                                                    ALU.mult, ALU.add)
                last.then_inc(acc_free[p], 1)

            dve.wait_ge(const_in, 16)
            dve.tensor_copy(ones[:, :], const[:, K_ONE:K_ONE + P]).then_inc(dve_step, 1)
            steps.step()
            dve.wait_ge(c_ok, 1)
            c_by = c_silu[:, :].rearrange("p (g k) -> p k g", g=2)
            step(dve.tensor_copy(c_parts[:, :, 0:2], c_by))
            settled()
            dve.tensor_tensor(c_parts[:, :, 2:4], c_by, f(c_parts[:, :, 0:2]), ALU.subtract).then_inc(rows_copied, 1)
            for kk in range(KD):
                pairs[kk % 2].step()
                square_parts(kk, kk % 2)

            def ffn(layer, s, with_ada, last_stage):
                if with_ada:
                    ada_low()
                for half in range(2):
                    q0 = half

                    def up(slot, j, smalls, last=False):
                        for hf in range(2):
                            u_t.step()
                            dve.wait_ge(acted_ok, u_t.at())
                            dve.tensor_tensor(prod[:, hf, 0, :], acted[:, hf, 0, :], acc[:, 2 * hf + 1, 0:HT], ALU.mult)\
                                .then_inc(acc_free[hf], 1)
                            pairs[hf].step()
                            freed(hf)
                            two_parts(u_hi[:, j, cols(hf)], u_lo[:, j, cols(hf)], prod[:, hf, 0, :], u_ready)
                            for n in range(smalls):
                                if not (half and last and hf and n):
                                    ada_low()
                        split(slot)

                    loops.repeat(HK // 2, lambda i: [up((q0 + e) % 2, i * 2 + e, int(with_ada)) for e in range(2)],
                                 unit=2, pair0=2, pair1=2, ada=4 * with_ada, u=4, steps=4)
                    up(q0, HK - 1, 2 * with_ada, True)

                    def down(n, e, more=True):
                        update_x(n, e, s)
                        if half:
                            square_parts(n, e)
                        if more:
                            split((q0 + 1 + e) % 2)
                    end = half == 1 and last_stage
                    loops.repeat(KD // 2 - end, lambda i: [down(i * 2 + e, e) for e in range(2)], unit=2,
                                 pair0=1, pair1=1, squares=2 * half, steps=2 * half)
                    if end:
                        for e in range(2):
                            down(KD - 2 + e, e, more=False)
                    if with_ada:
                        coefficients(half + 1, layer)

            def windows(g, b):
                w = WINDOWS[g]
                src, span = pf[:, b, :], 1
                for n in range(g + 1):
                    dst = win[n % 2]
                    step(dve.tensor_tensor(dst[:, 2 * span - 1:PW], src[:, 2 * span - 1:PW],
                                           src[:, span - 1:PW - span], ALU.add))
                    settled()
                    src, span = dst[:, :], 2 * span
                other = win[(g + 1) % 2]
                step(dve.tensor_tensor(first[:, :], src[:, HALO:HALO + 16],
                                       const[:, K_INV + 16 * g:K_INV + 16 * g + 16], ALU.mult))
                for a, n, c in ((HALO, TP, 0), (S0, TS, TP)):
                    step(dve.scalar_tensor_tensor(other[:, c:c + n], src[:, a:a + n], 1.0 / w, pf[:, b, a:a + n],
                                                  ALU.mult, ALU.subtract))
                settled()
                step(dve.tensor_tensor(other[:, 0:16], first[:, :], pf[:, b, HALO:HALO + 16], ALU.subtract))
                settled()
                two_parts(yp_hi[:, g, :], yp_lo[:, g, :], other[:, 0:T], yp_ready)

            def head(hd, layer):
                for b in range(JB):
                    sc_t.step()
                    dve.wait_ge(sc_ready, sc_t.at())
                    n = TP - b * P
                    dve.tensor_tensor(masked[:, b % 2, 0:n], const[:, K_MASK + hd * TP:K_MASK + hd * TP + n],
                                      (ps_mod, ps_misc)[b % 2][:, 0:n], ALU.mult).then_inc(masked_ok, 1)
                sc_t.step()
                dve.wait_ge(sc_ready, sc_t.at())
                dve.tensor_tensor(masked_s[0:TS, :], const[0:TS, K_MASK + hd * TP:K_MASK + hd * TP + TS],
                                  ps_sum[0:TS, 1, 0:TS], ALU.mult).then_inc(masked_ok, 1)
                dve.tensor_tensor(q_xi[:, :], q[:, hd, TP:T], const[:, K_XI + hd * TS:K_XI + (hd + 1) * TS],
                                  ALU.mult).then_inc(masked_ok, 1)
                pair0.step()
                dve.wait_ge(acc_ready[1], pair1.at(1))
                pair1.step()
                dve.wait_ge(s_out[hd % 2], layer * 64 + (32 * (hd // 2) + 32))
                dve.scalar_tensor_tensor(s_new[hd % 2][:, 1, :], s_old[:, hd, :], const[:, K_GBLK + hd:K_GBLK + hd + 1],
                                         acc[:, 3, 0:DK], ALU.mult, ALU.add)
                dve.tensor_copy(s_new[hd % 2][:, 0, :], acc[:, 2, 0:DK]).then_inc(acc_free[1], 1)

            def middle(layer):
                for kind, n in MID:
                    if kind == "qk":
                        for hf in range(2):
                            swap_t.step()
                            dve.wait_ge(swapped, swap_t.at())
                            z = tmp[:, hf, :].rearrange("p (a t) -> p a t", a=2)
                            for a, (dst, scale) in enumerate(((q, 1.0), (k, DK ** -0.5))):
                                step(dve.scalar_tensor_tensor(dst[:, n, cols(hf)], acc[:, 2 * hf + a, 0:HT], scale,
                                                              cos[:, cols(hf)], ALU.mult, ALU.mult))
                                step(dve.scalar_tensor_tensor(z[:, a], z[:, a], scale, sin[:, cols(hf)],
                                                              ALU.mult, ALU.mult))
                            settled()
                            for a, dst in enumerate((q, k)):
                                last = dve.tensor_tensor(dst[:, n, cols(hf)], dst[:, n, cols(hf)], z[:, a], ALU.add)
                            last.then_inc(acc_free[hf], 1)
                            pairs[hf].step()
                        split(n % 2)
                    elif kind == "v":
                        for t in range(TOK):
                            pairs[(n * TOK + t) % 2].step()
                        split(n)
                    elif kind == "pool":
                        if n:
                            tails.step()
                            dve.wait_ge(tails_t, tails.at())
                        step(dve.memset(pf[:, :, 0:HALO], 0.0))
                        cache = cache_t[:, :].rearrange("p (l t g) -> p l g t", l=DEPTH, g=GROUPS)
                        for b in range(2):
                            last = dve.tensor_copy(pf[:, b, HALO + TP:S0], cache[:, layer, 2 * n + b, :])
                        last.then_inc(halo_ready, 1)
                        for p in range(2):
                            pairs[p].step()
                        split(n)
                        dve.wait_ge(acc_free[1], pair1.at(1))
                        for b in range(2):
                            windows(2 * n + b, b)
                    elif kind == "map":
                        for e in range(2):
                            g = 2 * n + e
                            dve.wait_ge(acc_ready[e], pairs[e].at(1))
                            pairs[e].step()
                            dve.tensor_scalar(prod[:, e, :, :], pair_banks(e), vec_t[:, bass.ds(layer * R_ALL + (R_PS + g), 1)],
                                              None, ALU.mult).then_inc(acc_free[e], 1)
                            freed(e)
                            two_parts(halves(yp_hi[:, g, :]), halves(yp_lo[:, g, :]), prod[:, e, :, :], side_ready)
                        split(n)
                    elif kind == "head":
                        head(n, layer)
                    elif kind == "split":
                        y_t.step()
                        dve.wait_ge(y_copied, y_t.at(1))
                        two_parts(gn_hi[:, :], gn_lo[:, :], q[:, n, :], gn_split)
                    elif kind == "mean":
                        dve.wait_ge(acc_ready[0], pair0.at(1))
                        pair0.step()
                        y = halves(q[:, n, :])
                        dve.scalar_tensor_tensor(y, pair_banks(0), -1.0 / DK, y, ALU.mult, ALU.add)\
                            .then_inc(acc_free[0], 1)
                        sq_t.step()
                        dve.wait_ge(gn_squared, sq_t.at())
                        two_parts(gn_hi[:, :], gn_lo[:, :], tmp[:, 0, :], gn_split)
                    elif kind == "var":
                        pair1.step()
                        freed(1)
                        step(dve.reciprocal(rstd[:, :], rstd[:, :]))
                        settled()
                        step(dve.tensor_tensor(q[:, n, :], q[:, n, :], rstd[:, :], ALU.mult))
                    elif kind == "g":
                        settled()
                        for hf in range(2):
                            pairs[hf].step()
                            freed(hf)
                            for b in range(2):
                                hd = 2 * n + b
                                step(dve.scalar_tensor_tensor(prod[:, hf, b, :], q[:, hd, cols(hf)],
                                                              vec_t[:, bass.ds(layer * R_ALL + (R_GN + hd), 1)],
                                                              acted[:, hf, b, :], ALU.mult, ALU.mult))
                            settled()
                            two_parts(ry_hi[:, 2 * n:2 * n + 2, cols(hf)], ry_lo[:, 2 * n:2 * n + 2, cols(hf)],
                                      prod[:, hf, :, :], side_ready)
                        split(n)
                for mh in range(2):
                    def gate_out(i):
                        for p in range(2):
                            pairs[p].step()
                        split(0)
                        for hf in range(2):
                            dve.wait_ge(acc_ready[hf], pairs[hf].at(1))
                            pairs[hf].step()
                            dve.scalar_tensor_tensor(prod[:, hf, :, :], acted[:, hf, :, :], 1.0, pair_banks(hf),
                                                     ALU.add, ALU.mult).then_inc(acc_free[hf], 1)
                            freed(hf)
                            step(dve.tensor_tensor(prod[:, hf, 0, :], prod[:, hf, 0, :], prod[:, hf, 1, :], ALU.add))
                            settled()
                            two_parts(m_hi[:, i, cols(hf)], m_lo[:, i, cols(hf)], prod[:, hf, 0, :], side_ready)
                        split(1)
                    loops.repeat(4, gate_out, unit=2, pair0=2, pair1=2, steps=4)

                    def outs(i):
                        for e in range(2):
                            for b in range(2):
                                n = i * 4 + (2 * e + b)
                                update_x(n, b, 1)
                                if mh:
                                    square_parts(n, b)
                            split(e)
                    loops.repeat(2, outs, unit=2, pair0=2, pair1=2, squares=4 * mh, steps=4 * mh)

            def one_layer(layer):
                split(0)
                split(1)
                reciprocal_root()
                loops.repeat(CHUNKS, lambda i: [split(kh) for kh in range(2)], unit=2)
                coefficients(0, layer)
                make_h(0)
                ffn(layer, 0, True, False)
                reciprocal_root()
                make_h(1)
                middle(layer)
                reciprocal_root()
                make_h(2)
                ffn(layer, 2, False, True)
                tails.step()
                mask_t.step(24)
                gn_t.step(8)
                layers.step()
            loops.layers(one_layer)

            reciprocal_root()
            for kk in range(KD):
                dve.scalar_tensor_tensor(x[:, kk, :], x[:, kk, :], vec_t[:, R_FG + kk:R_FG + kk + 1], rstd[:, :],
                                         ALU.mult, ALU.mult).then_inc(h_ready, 1)


_INS = ["x_prompt", "x_sample", "c_prompt", "c_sample", "cache_pool", "state_ret", "w_ada", "b_ada", "norm_g",
        "w_up1", "w_down1", "w_up2", "w_down2", "w_in", "pool_map", "pool_scale", "w_pool_out", "ret_gn",
        "w_ret_out", "w_o", "final_g"]
_OUTS = [((1, TP, D), "float32"), ((1, TS, D), "float32"), ((DEPTH, 1, HALO, 512), "float32"),
         ((DEPTH, 1, HEADS, DK, DK), "float32"), ((DEPTH, 1, HALO, 512), "float32"),
         ((DEPTH, 1, HEADS, DK, DK), "float32")]


def constants():
    f32 = np.float32
    out = np.zeros((P, K_ALL), f32)
    out[:, K_ID:K_ID + P] = np.eye(P)
    out[:, K_ONE:K_ONE + P] = 1.0
    pos = np.concatenate([np.arange(TP), 1024 + np.arange(TS)]).astype(f32)
    inv = f32(10000.0) ** (-np.arange(64, dtype=f32) / f32(64))
    ang = (inv[:, None] * pos[None, :]).astype(f32).astype(np.float64)
    out[:, K_COS:K_COS + T] = np.tile(np.cos(ang), (2, 1))
    out[:, K_SIN:K_SIN + T] = np.concatenate([-np.sin(ang), np.sin(ang)])
    lg = np.log1p(-np.exp2(-5.0 - np.arange(HEADS)))
    p, c = np.arange(P)[:, None], np.arange(TP)[None, :]
    for h in range(HEADS):
        out[:, K_MASK + h * TP:K_MASK + (h + 1) * TP] = np.where(c >= p, np.exp(lg[h] * np.maximum(c - p, 0)), 0.0)
        out[:, K_XI + h * TS:K_XI + (h + 1) * TS] = np.exp(lg[h] * (np.arange(TS) + 1.0))
        for b in range(JB):
            out[:, K_ZETA + h * JB + b] = np.exp(lg[h] * (TP - 1.0 - b * P - np.arange(P)))
        out[:, K_ZETAS + h] = np.exp(lg[h] * np.maximum(TS - 1.0 - np.arange(P), 0))
        out[:, K_GBLK + h] = np.exp(lg[h] * TS)
    for g, w in enumerate(WINDOWS):
        out[:, K_INV + 16 * g:K_INV + 16 * (g + 1)] = 1.0 / np.minimum(w, np.arange(16) + 1.0)
    out[:, K_EPS] = EPS
    return out


def kernel(**inputs):
    import concourse.bacc as bacc
    from concourse.bass_utils import run_bass_kernel_spmd

    nc = bacc.Bacc("TRN2", target_bir_lowering=False, num_devices=1)
    arrays, args = {}, []
    for name in _INS:
        a = np.ascontiguousarray(inputs[name])
        arrays[f"in_{name}"] = a
        args.append(nc.dram_tensor(f"in_{name}", a.shape, mybir.dt.from_np(a.dtype), kind="ExternalInput").ap())
    arrays["in_consts"] = constants()
    args.append(nc.dram_tensor("in_consts", (P, K_ALL), F32, kind="ExternalInput").ap())
    for i, (shape, dtype) in enumerate(_OUTS):
        args.append(nc.dram_tensor(f"out_{i}", shape, mybir.dt.from_np(np.dtype(dtype)), kind="ExternalOutput").ap())
    trunk_kernel(nc, *args)
    r = run_bass_kernel_spmd(nc, [arrays], core_ids=[0])
    return tuple(r.results[0][f"out_{i}"] for i in range(len(_OUTS)))
```

```python
from contextlib import ExitStack

import numpy as np

import concourse.bass as bass
from concourse import mybir

ALU = mybir.AluOpType
ACT = mybir.ActivationFunctionType
F32 = mybir.dt.float32
F32R = mybir.dt.float32r

P = 128
D = 1024
TP, TS = 512, 32
T = TP + TS
HT = T // 2
KD = D // P
DEPTH = 2
FF = 2816
HK = FF // P // 2
HEADS, DK = 4, 128
GROUPS, HALO = 4, 15
WINDOWS = (2, 4, 8, 16)
PW = HALO + TP + HALO + TS
S0 = HALO + TP + HALO
SLOT = 2 * KD * P
EPS = 1e-6
N_MOD = 9
SETS = 3
CHUNKS = 6
JB = TP // P
TOK = JB + 1

C_POOL, C_Q, C_K, C_V, C_G, C_GATE = (512 * n for n in range(6))
PARTS = ((0, 0, HT, 0, 0), (1, 0, TP - HT, HT, 0), (1, TP - HT, HT, TP, 1))
SPANS = ((0, TP), (TP, T))

R_B, R_N, R_PS, R_GN, R_FG, R_ALL = 0, 72, 96, 100, 104, 112
R_CACHE = HALO * GROUPS

K_ID, K_ONE, K_COS, K_SIN, K_MASK = 0, 128, 256, 256 + T, 256 + 2 * T
K_XI = K_MASK + HEADS * TP
K_ZETA = K_XI + HEADS * TS
K_ZETAS = K_ZETA + HEADS * JB
K_GBLK = K_ZETAS + HEADS
K_INV = K_GBLK + HEADS
K_EPS = K_INV + GROUPS * 16
K_ALL = K_EPS + 1

UNITS = 128
PAIR0, PAIR1 = 111, 103
STEPS = 225
MID = (("pool", 0), ("w", 0), ("qk", 0), ("w", 1), ("win", 0), ("win", 1), ("v", 0), ("w", 0), ("qk", 1),
       ("head", 0), ("w", 1), ("split", 0), ("pool", 1), ("mean", 0), ("w", 0), ("qk", 2), ("var", 0), ("head", 1),
       ("w", 1), ("norm", 0), ("split", 1), ("win", 2), ("v", 1), ("mean", 1), ("w", 0), ("qk", 3), ("var", 1),
       ("head", 2), ("w", 1), ("norm", 1), ("split", 2), ("win", 3), ("g", 0), ("mean", 2), ("map", 0),
       ("var", 2), ("w", 0), ("head", 3), ("w", 1), ("gate", 0), ("norm", 2), ("split", 3), ("g", 1), ("ret", 0),
       ("mean", 3), ("w", 0), ("map", 1), ("var", 3), ("w", 1), ("norm", 3), ("gate", 1), ("ret", 1))
SLOTS = {}
for step_ in MID:
    if step_[0] in ("qk", "v", "pool", "map", "g"):
        SLOTS[step_] = len(SLOTS) % 2
NONE = (None, None)
SMALLS = ((0, 1), (2, 3))


class Tally:

    def __init__(self, each, start=0):
        self.each, self.start, self.n, self.layer, self.inner = each, start, 0, 0, 0

    def at(self, more=0):
        return self.layer * self.each + (self.inner + (self.start + self.n + more))

    def step(self, k=1):
        self.n += k


class Layers:

    def __init__(self, eng, tallies, passed):
        self.eng, self.tallies, self.passed = eng, tallies, passed

    def fence(self):
        self.eng.sem_inc(self.passed, 1)

    def layers(self, body):
        self.fence()
        with self.eng.Fori(0, DEPTH) as layer:
            for t in self.tallies:
                t.start, t.n, t.layer = t.start + t.n, 0, layer
            body(layer)
            for t in self.tallies:
                assert t.n == t.each, (t.name, t.n, t.each)
        for t in self.tallies:
            t.start, t.n, t.layer = t.start + DEPTH * t.each, 0, 0

    def repeat(self, count, body, **adds):
        before = {t: t.n for t in self.tallies}
        self.fence()
        with self.eng.Fori(0, count) as i:
            for t in self.tallies:
                t.inner = i * adds[t.name] if adds.get(t.name) else 0
            body(i)
            for t in self.tallies:
                assert t.n - before[t] == adds.get(t.name, 0), (t.name, t.n - before[t])
        for t in self.tallies:
            t.inner, t.n = 0, before[t] + count * adds.get(t.name, 0)


def halves(ap):
    return ap.rearrange("p (h t) -> p h t", h=2)


def trunk_kernel(nc, x_prompt, x_sample, c_prompt, c_sample, cache_pool, state_ret, w_ada, b_ada,
                 norm_g, w_up1, w_down1, w_up2, w_down2, w_in, pool_map, pool_scale, w_pool_out,
                 ret_gn, w_ret_out, w_o, final_g, consts,
                 y_prompt, y_sample, pool_prompt, ret_prompt, pool_sample, ret_sample):
    ctx = ExitStack()
    with ctx:
        def sb(name, shape, dt=F32, stack=ctx):
            return stack.enter_context(nc.sbuf_tensor(name, [P, *shape], dt))

        def sem(name):
            return ctx.enter_context(nc.semaphore(name))

        x = sb("x", [KD, T])
        h_hi, h_lo = sb("h_hi", [KD, T], F32R), sb("h_lo", [KD, T], F32R)
        raw = [sb(f"raw{p}", [SLOT]) for p in range(2)]
        w_hi = [sb(f"w_hi{p}", [SLOT], F32R) for p in range(2)]
        w_lo = [sb(f"w_lo{p}", [SLOT], F32R) for p in range(2)]
        const = sb("const", [K_ALL])
        ones = sb("ones", [P], F32R)
        vec_t = sb("vec_t", [DEPTH * R_ALL])
        cache_t = sb("cache_t", [DEPTH * R_CACHE])
        c_silu = sb("c_silu", [2 * KD])
        c_parts = sb("c_parts", [KD, 4], F32R)
        mod_t = sb("mod_t", [24, 4])
        mod_s = sb("mod_s", [24, 2])
        coef = sb("coef", [SETS, 3, KD, 2])
        s_old = sb("s_old", [HEADS, DK])
        s_new = [sb(f"s_new{p}", [2, DK]) for p in range(2)]
        tmp = sb("tmp", [2, T])
        rstd = sb("rstd", [T])
        acted = sb("acted", [2, 2, HT])
        prod = sb("prod", [2, 2, HT])

        with ExitStack() as st:
            rows_in = sb("rows_in", [DEPTH, 2, P], stack=st)
            x_in = sb("x_in", [TOK, D], stack=st)
            y_out = sb("y_out", [2, D], stack=st)
        with ExitStack() as st:
            mod_row = sb("mod_row", [CHUNKS, 512], stack=st)
            with ExitStack() as st2:
                raw += [sb(f"raw{p}", [SLOT], stack=st2) for p in (2, 3)]
                w_hi += [sb(f"w_hi{p}", [SLOT], F32R, st2) for p in (2, 3)]
                w_lo += [sb(f"w_lo{p}", [SLOT], F32R, st2) for p in (2, 3)]
            u_hi, u_lo = sb("u_hi", [HK, T], F32R, st), sb("u_lo", [HK, T], F32R, st)
            ada_raw = sb("ada_raw", [2, 512], stack=st)
            ada_hi, ada_lo = sb("ada_hi", [2, 512], F32R, st), sb("ada_lo", [2, 512], F32R, st)
        with ExitStack() as st:
            q = sb("q", [HEADS, T], stack=st)
            with ExitStack() as st2:
                k = sb("k", [HEADS, T], stack=st2)
                v = sb("v", [TOK, HEADS * DK], stack=st2)
                yp_hi, yp_lo = sb("yp_hi", [GROUPS, T], F32R, st2), sb("yp_lo", [GROUPS, T], F32R, st2)
                with ExitStack() as st3:
                    masked = sb("masked", [2, TP], stack=st3)
                    kz = sb("kz", [TOK, DK], stack=st3)
                    pf = sb("pf", [2, PW], stack=st3)
                    win = [sb(f"win{n}", [PW], stack=st3) for n in range(2)]
                    first = sb("first", [16], stack=st3)
                    gn_hi, gn_lo = sb("gn_hi", [T], F32R, st3), sb("gn_lo", [T], F32R, st3)
                    masked_s = sb("masked_s", [TS], stack=st3)
                    q_xi = sb("q_xi", [TS], stack=st3)
                    pool_rows = sb("pool_rows", [2, 512], stack=st3)
                m_hi, m_lo = sb("m_hi", [KD // 2, T], F32R, st2), sb("m_lo", [KD // 2, T], F32R, st2)
            ry_hi, ry_lo = sb("ry_hi", [HEADS, T], F32R, st), sb("ry_lo", [HEADS, T], F32R, st)

        acc = ctx.enter_context(nc.psum_tensor("acc", [P, 4, 512], F32))
        ps_mod = ctx.enter_context(nc.psum_tensor("ps_mod", [P, 512], F32))
        ps_misc = ctx.enter_context(nc.psum_tensor("ps_misc", [P, 512], F32))
        ps_sum = ctx.enter_context(nc.psum_tensor("ps_sum", [P, 2, 512], F32))

        ident = const[:, K_ID:K_ID + P]
        cos, sin = const[:, K_COS:K_COS + T], const[:, K_SIN:K_SIN + T]
        eps = const[:, K_EPS:K_EPS + 1]

        passed = sem("passed")
        ident_in = sem("ident_in")
        const_in = sem("const_in")
        rows_landed = sem("rows_landed")
        x_landed = sem("x_landed")
        raw_landed = [sem(f"raw_landed{p}") for p in range(4)]
        w_rounded = sem("w_rounded")
        w_split = sem("w_split")
        ada_landed = sem("ada_landed")
        ada_rounded = sem("ada_rounded")
        ada_split = sem("ada_split")
        ada_used = sem("ada_used")
        acc_ready = [sem(f"acc_ready{p}") for p in range(2)]
        acc_free = [sem(f"acc_free{p}") for p in range(2)]
        rows_t = sem("rows_t")
        rows_copied = sem("rows_copied")
        c_ok = sem("c_ok")
        mod_sum = sem("mod_sum")
        mod_copied = sem("mod_copied")
        mod_turned = sem("mod_turned")
        mod_cols = sem("mod_cols")
        acted_ok = sem("acted_ok")
        u_ready = sem("u_ready")
        x_squared = sem("x_squared")
        sq_split = sem("sq_split")
        sums_ready = sem("sums_ready")
        root_ok = sem("root_ok")
        scaled = sem("scaled")
        h_rounded = sem("h_rounded")
        h_ready = [sem(f"h_ready{p}") for p in range(2)]
        swapped = sem("swapped")
        halo_ready = sem("halo_ready")
        tails_t = sem("tails_t")
        tails_ok = sem("tails_ok")
        tails_out = sem("tails_out")
        doubled = sem("doubled")
        yp_ready = sem("yp_ready")
        sc_ready = sem("sc_ready")
        masked_ok = sem("masked_ok")
        y_ready = sem("y_ready")
        y_copied = sem("y_copied")
        s_landed = sem("s_landed")
        s_out = [sem(f"s_out{p}") for p in range(2)]
        gn_split = sem("gn_split")
        gn_squared = sem("gn_squared")
        side_ready = sem("side_ready")
        gated = sem("gated")
        out_copied = sem("out_copied")
        out_done = [sem(f"out_done{p}") for p in range(2)]
        dve_step = sem("dve_step")

        def pair_banks(p, columns=HT):
            return acc[:, 2 * p:2 * p + 2, 0:columns]

        def scaled_x(kk):
            return (tmp[:, 0, :], tmp[:, 1, :], prod[:, 0, :, :].rearrange("p a t -> p (a t)"),
                    prod[:, 1, :, :].rearrange("p a t -> p (a t)"))[kk % 4]

        def map_tile(g):
            return prod[:, g % 2, :, :].rearrange("p a t -> p (a t)")

        def load_vectors(eng, layer, landed):
            for r0, r1, t in ((R_B, R_N, b_ada[layer:layer + 1, :].rearrange("a (k f) -> (a k) f", f=P)),
                              (R_N, R_PS, norm_g[layer, :, :].rearrange("a (k f) -> (a k) f", f=P)),
                              (R_PS, R_GN, pool_scale[layer:layer + 1, :].rearrange("a (k f) -> (a k) f", f=P)),
                              (R_GN, R_FG, ret_gn[layer:layer + 1, :].rearrange("a (k f) -> (a k) f", f=P)),
                              (R_FG, R_ALL, final_g.rearrange("(k f) -> k f", f=P))):
                eng.dma_start(rows_in[r0:r1, layer, 0, :], t).then_inc(landed, 16)
            eng.dma_start(rows_in[0:R_CACHE, layer, 1, :],
                          cache_pool[layer, 0].rearrange("t (g f) -> (t g) f", f=P)).then_inc(landed, 16)

        block = ctx.enter_context(nc.Block())

        def tallies(**each):
            made = []
            for name, (n, start) in each.items():
                t = Tally(n, start)
                t.name = name
                made.append(t)
            return made

        @block.sync
        def _(sp):
            unit, = made = tallies(unit=(UNITS, 0))
            loops = Layers(sp, made, passed)

            for n, t in enumerate((c_prompt, c_sample)):
                sp.dma_start(rows_in[R_CACHE + n * KD:R_CACHE + (n + 1) * KD, 0, 1, :],
                             t.rearrange("a (k f) -> (a k) f", f=P)).then_inc(rows_landed, 16)
            load_vectors(sp, 0, rows_landed)

            def load(p, first_part, second_part, back=2):
                sp.wait_ge(w_split, unit.at(3 - back))
                loops.fence()
                for dst, src in (first_part, second_part):
                    sp.dma_start(dst, src).then_inc(raw_landed[p], 16)
                unit.step()

            def rows_of(w, layer):
                return w.rearrange("l (k p) n -> p l k n", p=P)[:, layer]

            def blocks(p, w, layer, c0, c1):
                to = raw[p][:, :].rearrange("p (b k n) -> p b k n", b=2, k=KD)
                load(p, (to[:, 0], rows_of(w, layer)[:, :, bass.ds(c0, P)]),
                     (to[:, 1], rows_of(w, layer)[:, :, bass.ds(c1, P)]))

            def rows(p, w, layer, k0, nk, c0, nc_, back=2):
                to = raw[p][:, 0:nk * nc_].rearrange("p (k n) -> p k n", k=nk)
                a = nk // 2
                load(p, (to[:, 0:a], rows_of(w, layer)[:, k0:k0 + a, bass.ds(c0, nc_)]),
                     (to[:, a:nk], rows_of(w, layer)[:, k0 + a:k0 + nk, bass.ds(c0, nc_)]), back)

            def ada_chunk(layer, c, slots, back=2):
                for kh in range(2):
                    rows(slots[kh], w_ada, layer, kh * 4, 4, c * 512, 512, back)

            def ffn(layer, w_up, w_down):
                for half in range(2):
                    j0 = half * HK
                    q0 = half
                    if w_up is w_up1:
                        ada_chunk(layer, (half + 1) * CHUNKS, (q0, 1 - q0), 2 if half else 4)

                    def up(i, p, j):
                        blocks(p, w_up, layer, j * P, j * P + FF)

                    def two_up(i):
                        for e in range(2):
                            up(i, (q0 + 1 + e) % 2, i * 2 + (j0 + 1 + e))
                    up(0, q0, j0)
                    loops.repeat(HK // 2, two_up, unit=2)

                    def two_down(i):
                        for e in range(2):
                            rows((q0 + 1 + e) % 2, w_down, layer, j0, HK, i * (2 * P) + e * P, P)
                    loops.repeat(KD // 2, two_down, unit=2)

            def layer_loads(layer):
                ada_chunk(layer, 0, (0, 1))
                sp.wait_ge(x_squared, layer * (SETS * KD) + KD)
                loops.fence()
                ada_chunk(layer, 1, (2, 3), 4)

                def two_chunks(i):
                    for e in range(2):
                        ada_chunk(layer, i * 2 + (2 + e), (2 * e, 2 * e + 1), 4)
                loops.repeat(CHUNKS // 2 - 1, two_chunks, unit=4)
                ffn(layer, w_up1, w_down1)
                sp.dma_start(s_old[:, :, :], state_ret.rearrange("l a h p n -> p l (a h) n")[:, layer])\
                    .then_inc(s_landed, 16)
                for kind, n in MID:
                    slot = SLOTS.get((kind, n))
                    if kind == "qk":
                        blocks(slot, w_in, layer, C_Q + n * P, C_K + n * P)
                    elif kind == "v":
                        rows(slot, w_in, layer, 0, KD, C_V + n * 256, 256)
                    elif kind == "pool":
                        blocks(slot, w_in, layer, C_POOL + n * 256, C_POOL + n * 256 + P)
                    elif kind == "map":
                        to = raw[slot][:, 0:2 * P].rearrange("p (g n) -> p g n", g=2)
                        src = pool_map.rearrange("l g p n -> p l g n")[:, layer]
                        load(slot, (to[:, 0:1], src[:, 2 * n:2 * n + 1]), (to[:, 1:2], src[:, 2 * n + 1:2 * n + 2]))
                    elif kind == "g":
                        blocks(slot, w_in, layer, C_G + n * 256, C_G + n * 256 + P)
                for mh in range(2):
                    def gate_out(i):
                        n = i * P + mh * 512
                        blocks(0, w_in, layer, C_GATE + n, C_GATE + D + n)
                        to = raw[1][:, 0:2 * 4 * P].rearrange("p (b k n) -> p b k n", b=2, k=4)
                        load(1, (to[:, 0], rows_of(w_pool_out, layer)[:, :, bass.ds(n, P)]),
                             (to[:, 1], rows_of(w_ret_out, layer)[:, :, bass.ds(n, P)]))
                    loops.repeat(4, gate_out, unit=2)

                    def outs(i):
                        for e in range(2):
                            rows(e, w_o, layer, 4 * mh, 4, i * 512 + e * 256, 256)
                    loops.repeat(2, outs, unit=2)
                ffn(layer, w_up2, w_down2)
            loops.layers(layer_loads)

            for t in range(TOK):
                sp.wait_ge(out_copied, t + 1)
                if t < JB:
                    sp.dma_start(y_prompt[0, t * P:(t + 1) * P, :], y_out[:, t % 2, :]).then_inc(out_done[t % 2], 16)
                else:
                    sp.dma_start(y_sample[0], y_out[0:TS, t % 2, :]).then_inc(out_done[t % 2], 16)
            sp.wait_ge(out_done[0], 16 * 3)
            sp.wait_ge(out_done[1], 16 * 2)

        @block.gpsimd
        def _(pool):
            def odd_h(s, layer):
                for n in range(KD // 2):
                    kk = 2 * n + 1
                    pool.wait_ge(h_rounded, layer * (SETS * KD) + (s * KD + kk + 1))
                    pool.tensor_tensor(h_lo[:, kk, :], scaled_x(kk), h_hi[:, kk, :].bitcast(F32), ALU.subtract)\
                        .then_inc(h_ready[1], 1)

            def square_parts(before):
                for n in range(KD):
                    pool.wait_ge(x_squared, before + (n + 1))
                    pool.tensor_tensor(h_lo[:, n, :], tmp[:, n % 2, :], h_hi[:, n, :].bitcast(F32), ALU.subtract)\
                        .then_inc(sq_split, 1)

            def window_sums(g, layer):
                pool.wait_ge(tails_ok, layer * 2 + (g // 2 + 1))
                if g:
                    pool.wait_ge(yp_ready, layer * GROUPS + g)
                src, span = pf[:, g % 2, :], 1
                for n in range(g + 1):
                    if n:
                        pool.wait_ge(doubled, layer * 10 + (g * (g + 1) // 2 + n))
                    dst = win[n % 2]
                    pool.tensor_tensor(dst[:, 2 * span - 1:PW], src[:, 2 * span - 1:PW], src[:, span - 1:PW - span],
                                       ALU.add).then_inc(doubled, 1)
                    src, span = dst[:, :], 2 * span

            square_parts(0)
            with pool.Fori(0, DEPTH) as layer:
                odd_h(0, layer)
                pool.sem_inc(passed, 1)
                with pool.Fori(0, 2) as half:
                    with pool.Fori(0, CHUNKS - 1) as c:
                        for kk in range(4):
                            pool.wait_ge(ada_split, layer * 40 + (half * 20 + (c * 4 + (kk + 1))))
                            pool.dma_start(ada_raw[:, :, :], w_ada.rearrange("l (k p) n -> p l k n", p=P)
                                           [:, layer, 2 * kk:2 * kk + 2,
                                            bass.ds(half * (CHUNKS * 512) + c * 512 + (CHUNKS + 1) * 512, 512)])\
                                .then_inc(ada_landed, 16)
                square_parts(layer * (SETS * KD) + KD)
                odd_h(1, layer)
                for g in range(GROUPS):
                    window_sums(g, layer)
                square_parts(layer * (SETS * KD) + 2 * KD)
                odd_h(2, layer)
                square_parts(layer * (SETS * KD) + 3 * KD)

        @block.tensor
        def _(pe):
            unit, ada, pair0, pair1, chunk, squares, h0, h1, u_t, tails, yp_t, mask_t, y_t, gn_t, side_t, layers = \
                made = tallies(unit=(UNITS, 0), ada=(40, 0), pair0=(PAIR0, 0), pair1=(PAIR1, 0), chunk=(18, 0),
                               squares=(24, 0), h=(12, 0), h1=(12, 0), u=(88, 0), tails=(2, 0), yp=(4, 0), mask=(24, 0),
                               y=(4, 0), gn=(8, 0), side=(24, 0), layers=(1, 0))
            pairs, hs = (pair0, pair1), (h0, h1)
            loops = Layers(pe, made, passed)

            mm = pe.matmul

            def begin_unit():
                pe.wait_ge(w_split, unit.at(1 + 2))
                unit.step()

            def take(p):
                pe.wait_ge(acc_free[p], pairs[p].at(1))

            def done(p, ins):
                ins.then_inc(acc_ready[p], 1)
                pairs[p].step()

            def product(out, ws, xs, nk):
                for kk in range(nk):
                    for n, (a, b) in enumerate(((0, 0), (0, 1), (1, 0))):
                        last = mm(out, ws(a, kk), xs(b, kk), start=(kk == 0 and n == 0),
                                  stop=(kk == nk - 1 and n == 2))
                return last

            def cols(hf):
                return slice(hf * HT, (hf + 1) * HT)

            def parts(hi, lo, hf):
                return lambda b, kk: (hi, lo)[b][:, kk, cols(hf)]

            def w_view(p, pattern, n, **sizes):
                return [t[p][:, 0:n].rearrange(pattern, **sizes) for t in (w_hi, w_lo)]

            def first_unit(p):
                begin_unit()
                w = w_view(p, "p (b k n) -> p b k n", SLOT, b=2, k=KD)
                take(0)
                take(1)
                for kk in range(KD):
                    hs[kk % 2].step()
                    pe.wait_ge(h_ready[kk % 2], hs[kk % 2].at())
                    for hf in range(2):
                        for b in range(2):
                            for n, (c, d) in enumerate(((0, 0), (0, 1), (1, 0))):
                                last = mm(acc[:, 2 * hf + b, 0:HT], w[c][:, b, kk, :], (h_hi, h_lo)[d][:, kk, cols(hf)],
                                          start=(kk == 0 and n == 0), stop=(kk == KD - 1 and n == 2))
                        if kk == KD - 1:
                            done(hf, last)

            def block_unit(p, smalls=NONE):
                begin_unit()
                w = w_view(p, "p (b k n) -> p b k n", SLOT, b=2, k=KD)
                for hf in range(2):
                    take(hf)
                    for b in range(2):
                        last = product(acc[:, 2 * hf + b, 0:HT], lambda a, kk: w[a][:, b, kk, :],
                                       parts(h_hi, h_lo, hf), KD)
                    done(hf, last)
                    if smalls[hf] is not None:
                        ada_small(smalls[hf])

            def ada_mm(kk, hi, lo, bank=ps_mod):
                for n, w in enumerate((hi, lo)):
                    last = mm(bank[0:4, :], c_parts[:, kk, :], w, start=(kk == 0 and n == 0),
                              stop=(kk == KD - 1 and n == 1))
                return last

            def ada_small(kp):
                if kp == 0:
                    pe.wait_ge(mod_copied, chunk.at(2))
                pe.wait_ge(ada_split, ada.at(1 + 1))
                for e in range(2):
                    last = ada_mm(2 * kp + e, ada_hi[:, e, :], ada_lo[:, e, :])
                ada.step()
                if kp == 3:
                    last.then_inc(mod_sum, 1)
                    chunk.step()
                else:
                    last.then_inc(ada_used, 1)

            def ada_big(bank, slots, back):
                for kh in range(2):
                    begin_unit()
                    w = w_view(slots[kh], "p (k n) -> p k n", SLOT, k=4)
                    if kh == 0:
                        pe.wait_ge(mod_copied, chunk.at(back))
                    for kk in range(4):
                        last = ada_mm(kh * 4 + kk, w[0][:, kk, :], w[1][:, kk, :], bank)
                    last.then_inc(mod_sum, 1)
                chunk.step()

            def turn_mods():
                pe.wait_ge(mod_copied, chunk.at(2))
                loops.fence()
                for j in range(24):
                    last = pe.matmul(ps_misc[:, 4 * j:4 * j + 4], mod_row[0:4, j // 4, (j % 4) * P:(j % 4 + 1) * P],
                                     ident[0:4, 0:4], is_transpose=True, start=True, stop=True)
                last.then_inc(mod_turned, 1)

            def column_sums(nk):
                for kk in range(nk):
                    pe.wait_ge(sq_split, squares.at(1 + 2))
                    squares.step()
                    for hf in range(2):
                        for b, part in enumerate((h_hi, h_lo)):
                            last = mm(ps_sum[:, hf, 0:HT], ones[:, :], part[:, kk, cols(hf)],
                                      start=(kk == 0 and b == 0), stop=(kk == nk - 1 and b == 1))
                last.then_inc(sums_ready, 1)

            pe.wait_ge(ident_in, 16)
            pe.wait_ge(x_landed, 16 * 2)
            for kk in range(KD):
                p = kk % 2
                take(p)
                for b in range(JB):
                    pe.matmul(acc[:, 2 * p, b * P:(b + 1) * P], x_in[:, b, kk * P:(kk + 1) * P], ident,
                              is_transpose=True, start=True, stop=True)
                done(p, pe.matmul(acc[:, 2 * p + 1, 0:TS], x_in[0:TS, JB, kk * P:(kk + 1) * P], ident[0:TS, 0:TS],
                                  is_transpose=True, start=True, stop=True))
            pe.wait_ge(rows_landed, 16 * (2 + 6 * DEPTH))
            for layer in range(DEPTH):
                pe.matmul(ps_misc[:, layer * 192:layer * 192 + R_ALL], rows_in[0:R_ALL, layer, 0, :],
                          ident[0:R_ALL, 0:R_ALL], is_transpose=True, start=True, stop=True)
                n = R_CACHE + (2 * KD if layer == 0 else 0)
                last = pe.matmul(ps_misc[:, layer * 192 + R_ALL:layer * 192 + R_ALL + n], rows_in[0:n, layer, 1, :],
                                 ident[0:n, 0:n], is_transpose=True, start=True, stop=True)
            last.then_inc(rows_t, 1)

            def ffn(with_ada):
                for half in range(2):
                    q0 = half

                    def two_up(i):
                        for e in range(2):
                            block_unit((q0 + 1 + e) % 2, SMALLS[e] if with_ada else NONE)
                    if with_ada:
                        ada_big(ps_mod, (q0, 1 - q0), 2)
                    if half == 0:
                        first_unit(q0)
                    else:
                        block_unit(q0)
                    n = int(with_ada)
                    loops.repeat(HK // 2, two_up, unit=2, pair0=2, pair1=2, ada=4 * n, chunk=n)
                    if with_ada:
                        turn_mods()
                    u_t.step(2 * HK)
                    pe.wait_ge(u_ready, u_t.at())

                    def two_down(i):
                        for e in range(2):
                            slot = (q0 + 1 + e) % 2
                            begin_unit()
                            w = w_view(slot, "p (k n) -> p k n", HK * P, k=HK)
                            take(e)
                            for hf in range(2):
                                last = product(acc[:, 2 * e + hf, 0:HT], lambda a, kk: w[a][:, kk, :],
                                               parts(u_hi, u_lo, hf), HK)
                            done(e, last)
                    loops.repeat(KD // 2, two_down, unit=2, pair0=1, pair1=1)

            def head(hd):
                own = slice(hd * DK, (hd + 1) * DK)
                take(0)
                pe.wait_ge(acc_free[1], pair1.at(0))
                for b in range(JB):
                    pe.matmul(acc[:, 0, b * P:(b + 1) * P], k[:, hd, b * P:(b + 1) * P], ident,
                              is_transpose=True, start=True, stop=True)
                done(0, pe.matmul(acc[0:TS, 1, 0:P], k[:, hd, TP:T], ident, is_transpose=True, start=True, stop=True))

                bank = (ps_mod, ps_misc)

                def scores(b):
                    pe.matmul(bank[b % 2][:, 0:TP - b * P], k[:, hd, b * P:(b + 1) * P], q[:, hd, b * P:TP],
                              start=True, stop=True).then_inc(sc_ready, 1)

                def values(b):
                    mask_t.step()
                    pe.wait_ge(masked_ok, mask_t.at())
                    pe.matmul(ps_sum[:, 0, b * P:TP], v[:, b, own], masked[:, b % 2, 0:TP - b * P],
                              start=(b == 0), stop=(b == JB - 1))

                if hd == 0:
                    layers.step()
                    pe.wait_ge(s_landed, layers.at() * 16)
                scores(0)
                if hd < 2:
                    tails.step()
                    pe.wait_ge(tails_ok, tails.at())
                scores(1)
                pe.wait_ge(y_copied, y_t.at(1))
                values(0)
                scores(2)
                values(1)
                scores(3)
                values(2)
                pe.matmul(ps_sum[0:TS, 1, 0:TS], k[:, hd, TP:T], q[:, hd, TP:T], start=True, stop=True)\
                    .then_inc(sc_ready, 1)
                values(3)
                mask_t.step(2)
                pe.wait_ge(masked_ok, mask_t.at())
                pe.matmul(ps_sum[:, 1, 64:64 + TS], v[0:TS, JB, own], masked_s[0:TS, :], start=True, stop=False)
                pe.matmul(ps_sum[:, 1, 64:64 + TS], s_old[:, hd, :], q_xi[:, :], start=False, stop=True)\
                    .then_inc(y_ready, 1)
                y_t.step()
                pe.wait_ge(acc_free[0], pair0.at(1))
                take(1)
                for b in range(JB):
                    pe.matmul(acc[:, 2, 0:DK], kz[:, b, :], v[:, b, own], start=(b == 0), stop=(b == JB - 1))
                done(1, pe.matmul(acc[:, 3, 0:DK], kz[0:TS, JB, :], v[0:TS, JB, own], start=True, stop=True))

            def group_sum():
                gn_t.step()
                pe.wait_ge(gn_split, gn_t.at())
                take(0)
                for hf in range(2):
                    for b, part in enumerate((gn_hi, gn_lo)):
                        last = pe.matmul(acc[:, hf, 0:HT], ones[:, :], part[:, cols(hf)],
                                         start=(b == 0), stop=(b == 1))
                done(0, last)

            def middle():
                for kind, n in MID:
                    slot = SLOTS.get((kind, n))
                    if (kind, n) == MID[0]:
                        first_unit(slot)
                    elif kind in ("qk", "g", "pool"):
                        block_unit(slot)
                    if kind == "pool":
                        pe.wait_ge(acc_free[1], pair1.at(1))
                        for s, c0 in enumerate((HALO + TP - HALO, PW - HALO)):
                            for b in range(2):
                                last = pe.matmul(ps_misc[0:HALO, (2 * s + b) * P:(2 * s + b + 1) * P],
                                                 pf[:, b, c0:c0 + HALO], ident, is_transpose=True, start=True,
                                                 stop=True)
                        last.then_inc(tails_t, 1)
                    elif kind == "v":
                        begin_unit()
                        w = w_view(slot, "p (k n) -> p k n", SLOT, k=KD)
                        for t in range(TOK):
                            p = (n * TOK + t) % 2
                            rows = P if t < JB else TS
                            take(p)
                            done(p, product(acc[0:rows, 2 * p, 0:256],
                                            lambda a, kk: (h_hi, h_lo)[a][:, kk, t * P:t * P + rows],
                                            lambda b, kk: w[b][:, kk, :], KD))
                    elif kind == "map":
                        begin_unit()
                        w = w_view(slot, "p (g n) -> p g n", 2 * P, g=2)
                        for e in range(2):
                            g = 2 * n + e
                            yp_t.step()
                            pe.wait_ge(yp_ready, yp_t.at())
                            take(e)
                            for hf in range(2):
                                last = product(acc[:, 2 * e + hf, 0:HT], lambda a, kk: w[a][:, e, :],
                                               lambda b, kk: (yp_hi, yp_lo)[b][:, g, cols(hf)], 1)
                            done(e, last)
                    elif kind == "head":
                        head(n)
                    elif kind in ("mean", "var"):
                        group_sum()
                side_t.step(4 + 4)
                for mh in range(2):
                    def gate_out(i):
                        block_unit(0)
                        pe.wait_ge(side_ready, side_t.at())
                        begin_unit()
                        w = w_view(1, "p (b k n) -> p b k n", 2 * 4 * P, b=2, k=4)
                        for hf in range(2):
                            take(hf)
                            product(acc[:, 2 * hf, 0:HT], lambda a, kk: w[a][:, 0, kk, :], parts(yp_hi, yp_lo, hf), 4)
                            done(hf, product(acc[:, 2 * hf + 1, 0:HT], lambda a, kk: w[a][:, 1, kk, :],
                                             parts(ry_hi, ry_lo, hf), 4))
                    loops.repeat(4, gate_out, unit=2, pair0=2, pair1=2)
                    side_t.step(8)
                    pe.wait_ge(side_ready, side_t.at(-2))

                    def outs(i):
                        for e in range(2):
                            begin_unit()
                            w = w_view(e, "p (k n) -> p k n", 4 * 256, k=4)
                            for b in range(2):
                                take(b)
                                for kk in range(4):
                                    if kk == 3:
                                        pe.wait_ge(side_ready, side_t.at())
                                    for hf in range(2):
                                        for n, (c, d) in enumerate(((0, 0), (0, 1), (1, 0))):
                                            last = mm(acc[:, 2 * b + hf, 0:HT], w[c][:, kk, b * P:(b + 1) * P],
                                                      (m_hi, m_lo)[d][:, kk, cols(hf)],
                                                      start=(kk == 0 and n == 0), stop=(kk == 3 and n == 2))
                                done(b, last)
                    loops.repeat(2, outs, unit=2, pair0=2, pair1=2)

            def one_layer(layer):
                column_sums(KD)

                loops.repeat(CHUNKS // 2, lambda i: [ada_big(ps_mod, (0, 1), 1), ada_big(ps_misc, (2, 3), 1)],
                             unit=4, chunk=2)
                turn_mods()
                ffn(True)
                column_sums(KD)
                middle()
                column_sums(KD)
                ffn(False)
            pe.wait_ge(rows_copied, 5)
            loops.layers(one_layer)

            column_sums(KD)
            h0.step(KD)
            pe.wait_ge(h_ready[0], h0.at())
            for t in range(TOK):
                p, rows = t % 2, (P if t < JB else TS)
                if t < 2:
                    take(p)
                else:
                    pe.wait_ge(out_copied, t - 1)
                for kk in range(KD):
                    last = pe.matmul(acc[0:rows, 2 * p + kk // 4, (kk % 4) * P:(kk % 4 + 1) * P],
                                     x[:, kk, t * P:t * P + rows], ident, is_transpose=True, start=True, stop=True)
                done(p, last)

        @block.scalar
        def _(act):
            land0, land1, land2, land3, ada, used, pair0, pair1, chunk, sets, norms, squares, scale_t, pf_t, y_t, \
                gated_t, gn_t = made = tallies(
                               land0=(UNITS // 2 - 3, 0), land1=(UNITS // 2 - 3, 0), land2=(3, 0), land3=(3, 0),
                               ada=(40, 0), used=(30, 0), pair0=(PAIR0, 0), pair1=(PAIR1, 0), chunk=(26, 0),
                               sets=(3, 0), norms=(3, 0), squares=(24, 0), scale=(24, 0), pf=(2, 0), y=(4, 0),
                               gated=(4, 0), gn=(8, 0))
            pairs, lands = (pair0, pair1), (land0, land1, land2, land3)
            loops = Layers(act, made, passed)

            act.sem_inc(mod_copied, 2)
            act.sem_inc(y_copied, 1)
            act.sem_inc(tails_out, 32)
            for p in range(2):
                act.sem_inc(s_out[p], 32)
            for p in range(2):
                act.sem_inc(acc_free[p], 1)

            act.dma_start(const[:, 0:K_COS], consts[:, 0:K_COS]).then_inc(ident_in, 16)
            act.dma_start(x_in[:, 0:JB, :], x_prompt[0].rearrange("(b p) f -> p b f", p=P)).then_inc(x_landed, 16)
            act.dma_start(x_in[0:TS, JB, :], x_sample[0]).then_inc(x_landed, 16)

            load_vectors(act, 1, rows_landed)
            act.dma_start(const[:, K_COS:K_ALL], consts[:, K_COS:K_ALL]).then_inc(const_in, 16)

            def split(p):
                act.wait_ge(raw_landed[p], lands[p].at(1) * 32)
                act.activation(w_hi[p][:, :], raw[p][:, :], ACT.Copy).then_inc(w_rounded, 1)
                lands[p].step()

            def ada_high():
                act.wait_ge(ada_landed, ada.at(1) * 16)
                act.activation(ada_hi[:, :, :], ada_raw[:, :, :], ACT.Copy).then_inc(ada_rounded, 1)
                ada.step()

            def copy_row(row, bank=ps_mod):
                chunk.step()
                act.wait_ge(mod_sum, chunk.at())
                act.activation(mod_row[0:4, row, :], bank[0:4, :], ACT.Copy).then_inc(mod_copied, 1)

            def used_chunk():
                chunk.step()
                act.wait_ge(mod_sum, chunk.at())

            def big_row(row, bank, slots):
                used_chunk()
                if slots:
                    split(slots[0])
                copy_row(row, bank)
                if slots:
                    split(slots[1])

            def wait_group(p):
                act.wait_ge(acc_ready[p], pairs[p].at(1))
                pairs[p].step()

            def copy_mods():
                sets.step()
                act.wait_ge(mod_turned, sets.at())
                act.activation(mod_t[:, :, :].rearrange("p a b -> p (a b)"), ps_misc[:, 0:96], ACT.Copy)\
                    .then_inc(mod_cols, 1)

            def square(n, par, x_new):
                act.wait_ge(*x_new)
                act.wait_ge(sq_split, squares.at(1))
                act.activation(tmp[:, par, :], x[:, n, :], ACT.Square)
                act.activation(h_hi[:, n, :], x[:, n, :], ACT.Square).then_inc(x_squared, 1)
                squares.step()

            def norm_root():
                norms.step()
                act.wait_ge(sums_ready, norms.at())
                act.activation(halves(rstd[:, :]), ps_sum[:, :, 0:HT], ACT.Sqrt, scale=1.0 / D, bias=eps)\
                    .then_inc(root_ok, 1)

            def round_h(s, kk):
                scale_t.step()
                act.wait_ge(scaled, scale_t.at())
                for g, (a, b) in enumerate(SPANS):
                    last = act.activation(h_hi[:, kk, a:b], scaled_x(kk)[:, a:b], ACT.Identity,
                                          bias=coef[:, s, 0, kk, g:g + 1], scale=1.0)
                if kk % 2:
                    for g, (a, b) in enumerate(SPANS):
                        last = act.activation(scaled_x(kk)[:, a:b], scaled_x(kk)[:, a:b], ACT.Identity,
                                              bias=coef[:, s, 0, kk, g:g + 1], scale=1.0)
                last.then_inc(h_rounded, 1)

            for kk in range(KD):
                pairs[kk % 2].step()
                square(kk, kk % 2, (acc_free[kk % 2], pairs[kk % 2].at(1)))
            act.wait_ge(rows_t, 1)
            for layer in range(DEPTH):
                o = layer * 192
                act.activation(vec_t[:, layer * R_ALL:(layer + 1) * R_ALL], ps_misc[:, o:o + R_ALL], ACT.Copy)\
                    .then_inc(rows_copied, 1)
                act.activation(cache_t[:, layer * R_CACHE:(layer + 1) * R_CACHE],
                               ps_misc[:, o + R_ALL:o + R_ALL + R_CACHE], ACT.Copy).then_inc(rows_copied, 1)
            act.activation(c_silu[:, :], ps_misc[:, R_ALL + R_CACHE:R_ALL + R_CACHE + 2 * KD], ACT.Silu)\
                .then_inc(c_ok, 1)
            act.wait_ge(const_in, 16)

            def down_steps(n, p, last_half):
                wait_group(p)
                if last_half:
                    square(n, p, (acc_free[p], pairs[p].at(1)))

            def ffn(with_ada, last_stage):
                for half in range(2):
                    q0 = half

                    def run(smalls, row):
                        for hf in range(2):
                            wait_group(hf)
                            act.activation(acted[:, hf, 0, :], acc[:, 2 * hf, 0:HT], ACT.Silu).then_inc(acted_ok, 1)
                            if smalls[hf] == 3:
                                copy_row(row)
                            elif smalls[hf] is not None:
                                used.step()
                                act.wait_ge(ada_used, used.at())
                                ada_high()

                    def two_up(i):
                        if with_ada:
                            ada_high()
                        for e in range(2):
                            split((q0 + e) % 2)
                            run(SMALLS[e] if with_ada else NONE, i + 1)
                    if half == 0 and with_ada:
                        for kk in range(KD):
                            round_h(0, kk)
                            if kk == 1:
                                used_chunk()
                            elif kk == 2:
                                split(q0)
                            elif kk == 3:
                                copy_row(0)
                        split(1 - q0)
                    elif half == 0:
                        for kk in range(KD):
                            round_h(2, kk)
                    elif with_ada:
                        big_row(0, ps_mod, (q0, 1 - q0))
                    n = int(with_ada)
                    run(NONE, 0)
                    loops.repeat(HK // 2, two_up, land0=1, land1=1, pair0=2, pair1=2, ada=4 * n,
                                 used=3 * n, chunk=n)
                    split(q0)
                    if with_ada:
                        copy_mods()

                    def down(n, e, more=True):
                        down_steps(n, e, half == 1)
                        if more:
                            split((q0 + 1 + e) % 2)
                    end = half == 1 and last_stage
                    turns = KD // 2 - (1 if end else 0)
                    loops.repeat(turns, lambda i: [down(i * 2 + e, e) for e in range(2)], land0=1, land1=1,
                                 pair0=1, pair1=1, squares=2 * half)
                    if end:
                        for e in range(2):
                            down(KD - 2 + e, e, more=False)
            def middle():
                def head(hd):
                    wait_group(0)
                    for b in range(JB):
                        act.activation(kz[:, b, :], acc[:, 0, b * P:(b + 1) * P], ACT.Copy,
                                       scale=const[:, K_ZETA + hd * JB + b:K_ZETA + hd * JB + b + 1])
                    act.activation(kz[0:TS, JB, :], acc[0:TS, 1, 0:P], ACT.Copy,
                                   scale=const[0:TS, K_ZETAS + hd:K_ZETAS + hd + 1]).then_inc(acc_free[0], 1)
                    y_t.step()
                    act.wait_ge(y_ready, y_t.at())
                    act.activation(q[:, hd, 0:TP], ps_sum[:, 0, :], ACT.Copy)
                    act.activation(q[:, hd, TP:T], ps_sum[:, 1, 64:64 + TS], ACT.Copy).then_inc(y_copied, 1)
                    pairs[1].step()
                    act.wait_ge(acc_free[1], pair1.at(1))
                    act.dma_start(ret_prompt.rearrange("l a h p n -> p l (a h) n")[:, loops.layer, hd, :],
                                  s_new[hd % 2][:, 0, :]).then_inc(s_out[hd % 2], 16)
                    act.dma_start(ret_sample.rearrange("l a h p n -> p l (a h) n")[:, loops.layer, hd, :],
                                  s_new[hd % 2][:, 1, :]).then_inc(s_out[hd % 2], 16)

                for kind, n in MID:
                    if kind == "w":
                        split(n)
                    if kind in ("split", "mean"):
                        gn_t.step()
                    if kind == "qk":
                        if n >= 2:
                            act.wait_ge(gn_split, gn_t.at())
                        for hf in range(2):
                            wait_group(hf)
                            z = tmp[:, hf, :].rearrange("p (a t) -> p a t", a=2)
                            act.activation(z[64:128], acc[0:64, 2 * hf:2 * hf + 2, 0:HT], ACT.Copy)
                            act.activation(z[0:64], acc[64:128, 2 * hf:2 * hf + 2, 0:HT], ACT.Copy)\
                                .then_inc(swapped, 1)
                    elif kind == "v":
                        for t in range(TOK):
                            p, rows = (n * TOK + t) % 2, (P if t < JB else TS)
                            wait_group(p)
                            act.activation(v[0:rows, t, n * 256:(n + 1) * 256], acc[0:rows, 2 * p, 0:256], ACT.Copy)\
                                .then_inc(acc_free[p], 1)
                    elif kind == "pool":
                        pf_t.step()
                        act.wait_ge(halo_ready, pf_t.at())
                        for hf in range(2):
                            wait_group(hf)
                            if hf == 0:
                                act.activation(pf[:, :, HALO:HALO + HT], pair_banks(0), ACT.Copy)\
                                    .then_inc(acc_free[0], 1)
                            else:
                                act.activation(pf[:, :, HALO + HT:HALO + TP], acc[:, 2:4, 0:TP - HT], ACT.Copy)
                                act.activation(pf[:, :, S0:PW], acc[:, 2:4, TP - HT:HT], ACT.Copy)\
                                    .then_inc(acc_free[1], 1)
                        act.wait_ge(tails_t, pf_t.at())
                        for s in range(2):
                            last = act.activation(pool_rows[0:HALO, s, n * 256:(n + 1) * 256],
                                                  ps_misc[0:HALO, s * 256:(s + 1) * 256], ACT.Copy)
                        last.then_inc(tails_ok, 1)
                        if n == 1:
                            act.wait_ge(tails_ok, pf_t.at())
                            for s, out in enumerate((pool_prompt, pool_sample)):
                                act.dma_start(out.rearrange("l a t f -> t l (a f)")[:, loops.layer, :],
                                              pool_rows[0:HALO, s, :]).then_inc(tails_out, 16)
                    elif kind == "map":
                        for e in range(2):
                            wait_group(e)
                            act.activation(halves(map_tile(2 * n + e)), pair_banks(e), ACT.Copy,
                                           scale=vec_t[:, bass.ds(loops.layer * R_ALL + (R_PS + 2 * n + e), 1)])\
                                .then_inc(acc_free[e], 1)
                    elif kind == "head":
                        head(n)
                    elif kind == "mean":
                        pairs[0].step()
                        act.wait_ge(acc_free[0], pair0.at(1))
                        act.activation(tmp[:, 0, :], q[:, n, :], ACT.Square).then_inc(gn_squared, 1)
                    elif kind == "var":
                        wait_group(0)
                        act.activation(halves(rstd[:, :]), pair_banks(0), ACT.Sqrt, scale=1.0 / DK, bias=eps)\
                            .then_inc(acc_free[0], 1)
                    elif kind == "g":
                        for hf in range(2):
                            wait_group(hf)
                            if n:
                                act.wait_ge(gated, gated_t.at(1))
                                gated_t.step()
                            act.activation(acted[:, hf, :, :], pair_banks(hf), ACT.Silu).then_inc(acc_free[hf], 1)

                gated_t.step(2)
                act.wait_ge(gated, gated_t.at())
                for mh in range(2):
                    def gate_out(i):
                        for hf in range(2):
                            wait_group(hf)
                            act.activation(acted[:, hf, :, :], pair_banks(hf), ACT.Tanh, scale=0.5)\
                                .then_inc(acc_free[hf], 1)
                        split(0)
                        for hf in range(2):
                            wait_group(hf)
                        split(1)
                    loops.repeat(4, gate_out, land0=1, land1=1, pair0=2, pair1=2)

                    def outs(i):
                        for e in range(2):
                            n = i * 4 + 2 * e
                            down_steps(n, 0, mh == 1)
                            wait_group(1)
                            split(e)
                            if mh:
                                square(n + 1, 1, (acc_free[1], pair1.at(1)))
                    loops.repeat(2, outs, land0=1, land1=1, pair0=2, pair1=2, squares=4 * mh)

            def one_layer(layer):
                loops.layer = layer
                split(0)
                split(1)
                norm_root()
                split(2)
                split(3)

                def ada_rows(i):
                    for e, bank in enumerate((ps_mod, ps_misc)):
                        big_row(i * 2 + e, bank, (2 * e, 2 * e + 1))
                loops.repeat(CHUNKS // 2 - 1, ada_rows, land0=1, land1=1, land2=1, land3=1, chunk=4)
                big_row(CHUNKS - 2, ps_mod, (0, 1))
                big_row(CHUNKS - 1, ps_misc, None)
                copy_mods()
                ffn(True, False)
                norm_root()
                for kk in range(KD):
                    round_h(1, kk)
                middle()
                norm_root()
                ffn(False, True)
                act.wait_ge(tails_out, layer * 32 + 64)
            loops.layers(one_layer)

            norm_root()
            for t in range(TOK):
                p, rows = t % 2, (P if t < JB else TS)
                wait_group(p)
                if t >= 2:
                    act.wait_ge(out_done[p], 16 * (t // 2))
                act.activation(y_out[0:rows, p, :].rearrange("p (b n) -> p b n", b=2), acc[0:rows, 2 * p:2 * p + 2, :],
                               ACT.Copy).then_inc(out_copied, 1)
            act.wait_ge(tails_out, 32 * DEPTH + 32)
            for p in range(2):
                act.wait_ge(s_out[p], 64 * DEPTH + 32)

        @block.vector
        def _(dve):
            unit, ada, pair0, pair1, sets, norms, h_t, odd_t, rounded_t, u_t, swap_t, tails, mask_t, sc_t, y_t, \
                gn_t, sq_t, sums_t, gated_t, steps, layers = made = tallies(
                    unit=(UNITS, 0), ada=(40, 0), pair0=(PAIR0, 0), pair1=(PAIR1, 0), sets=(3, 0), norms=(3, 0),
                    h=(12, 0), odd=(12, 0), rounded=(24, 0), u=(88, 0), swap=(8, 0), tails=(2, 0), mask=(24, 0),
                    sc=(20, 0), y=(4, 0), gn=(8, 0), sq=(4, 0), sums=(10, 0), gated=(4, 0), steps=(STEPS, 0),
                    layers=(1, 0))
            pairs = (pair0, pair1)
            loops = Layers(dve, made, passed)

            dve.sem_inc(w_split, 2)
            dve.sem_inc(ada_split, 1)
            dve.sem_inc(sq_split, 2)

            def step(ins):
                ins.then_inc(dve_step, 1)
                steps.step()

            def settled():
                dve.wait_ge(dve_step, steps.at())

            def f(ap):
                return ap.bitcast(F32)

            def cols(hf):
                return slice(hf * HT, (hf + 1) * HT)

            def two_parts(hi, lo, src, done):
                step(dve.tensor_copy(hi, src))
                settled()
                dve.tensor_tensor(lo, src, f(hi), ALU.subtract).then_inc(done, 1)

            def freed(p):
                dve.wait_ge(acc_free[p], pairs[p].at(1))

            def split(p):
                dve.wait_ge(w_rounded, unit.at(1))
                dve.tensor_tensor(w_lo[p][:, :], raw[p][:, :], f(w_hi[p][:, :]), ALU.subtract).then_inc(w_split, 1)
                unit.step()

            def ada_low():
                dve.wait_ge(ada_rounded, ada.at(1))
                dve.tensor_tensor(ada_lo[:, :, :], ada_raw[:, :, :], f(ada_hi[:, :, :]), ALU.subtract)\
                    .then_inc(ada_split, 1)
                ada.step()

            def coefficients(s, layer):
                sets.step()
                dve.wait_ge(mod_cols, sets.at())
                for g in range(2):
                    step(dve.scalar_tensor_tensor(mod_s[:, :, g], mod_t[:, :, g], 1.0, mod_t[:, :, 2 + g],
                                                  ALU.mult, ALU.add))
                settled()
                o = layer * R_ALL
                for g in range(2):
                    step(dve.tensor_tensor(mod_s[:, :, g], mod_s[:, :, g], vec_t[:, bass.ds(o + (R_B + 24 * s), 24)],
                                           ALU.add))
                settled()
                step(dve.tensor_copy(coef[:, s, 0, :, :], mod_s[:, 0:KD, :]))
                for g in range(2):
                    step(dve.scalar_tensor_tensor(coef[:, s, 1, :, g], mod_s[:, KD:2 * KD, g], 1.0,
                                                  vec_t[:, bass.ds(o + (R_N + KD * s), KD)], ALU.add, ALU.mult))
                step(dve.tensor_scalar(coef[:, s, 2, :, :], mod_s[:, 2 * KD:, :], 0.5, None, ALU.mult))
                settled()

            def reciprocal_root():
                norms.step()
                dve.wait_ge(root_ok, norms.at())
                step(dve.reciprocal(rstd[:, :], rstd[:, :]))
                settled()

            def make_h(s, slot=None):
                def scale(kk):
                    for g, (a, b) in enumerate(SPANS):
                        last = dve.scalar_tensor_tensor(scaled_x(kk)[:, a:b], x[:, kk, a:b],
                                                        coef[:, s, 1, kk, g:g + 1], rstd[:, a:b], ALU.mult, ALU.mult)
                    last.then_inc(scaled, 1)
                scale(0)
                for kk in range(0, KD, 2):
                    if kk >= 4:
                        dve.wait_ge(h_ready[1], odd_t.at(kk // 2 - 1))
                    scale(kk + 1)
                    if kk + 2 < KD:
                        if kk >= 2:
                            dve.wait_ge(h_ready[0], h_t.at())
                        scale(kk + 2)
                    h_t.step()
                    rounded_t.step()
                    dve.wait_ge(h_rounded, rounded_t.at())
                    rounded_t.step()
                    for g, (a, b) in enumerate(SPANS):
                        last = dve.scalar_tensor_tensor(h_lo[:, kk, a:b], scaled_x(kk)[:, a:b],
                                                        coef[:, s, 0, kk, g:g + 1], f(h_hi[:, kk, a:b]),
                                                        ALU.add, ALU.subtract)
                    last.then_inc(h_ready[0], 1)
                    if kk == 2 and slot is not None:
                        split(slot)
                odd_t.step(KD // 2)
                dve.wait_ge(h_ready[1], odd_t.at())

            def update_x(n, p, s):
                dve.wait_ge(acc_ready[p], pairs[p].at(1))
                pairs[p].step()
                for hf, a, b, c, g in PARTS:
                    last = dve.scalar_tensor_tensor(x[:, n, c:c + b - a], acc[:, 2 * p + hf, a:b],
                                                    coef[:, s, 2, n, g:g + 1], x[:, n, c:c + b - a],
                                                    ALU.mult, ALU.add)
                last.then_inc(acc_free[p], 1)

            dve.wait_ge(ident_in, 16)
            dve.tensor_copy(ones[:, :], const[:, K_ONE:K_ONE + P]).then_inc(dve_step, 1)
            steps.step()
            for kk in range(KD):
                p = kk % 2
                dve.wait_ge(acc_ready[p], pairs[p].at(1))
                pairs[p].step()
                dve.tensor_copy(x[:, kk, 0:TP], acc[:, 2 * p, :])
                dve.tensor_copy(x[:, kk, TP:T], acc[:, 2 * p + 1, 0:TS]).then_inc(acc_free[p], 1)
            dve.wait_ge(c_ok, 1)
            c_by = c_silu[:, :].rearrange("p (g k) -> p k g", g=2)
            step(dve.tensor_copy(c_parts[:, :, 0:2], c_by))
            settled()
            dve.tensor_tensor(c_parts[:, :, 2:4], c_by, f(c_parts[:, :, 0:2]), ALU.subtract).then_inc(rows_copied, 1)
            dve.wait_ge(const_in, 16)

            def ffn(layer, s, with_ada, last_stage):
                for half in range(2):
                    q0 = half
                    if half == 0:
                        make_h(s, q0 if with_ada else None)
                    elif with_ada:
                        split(q0)
                    if with_ada:
                        split(1 - q0)

                    def up(j, smalls):
                        for hf in range(2):
                            u_t.step()
                            dve.wait_ge(acted_ok, u_t.at())
                            dve.tensor_tensor(prod[:, hf, 0, :], acted[:, hf, 0, :], acc[:, 2 * hf + 1, 0:HT],
                                              ALU.mult).then_inc(acc_free[hf], 1)
                            pairs[hf].step()
                            freed(hf)
                            two_parts(u_hi[:, j, cols(hf)], u_lo[:, j, cols(hf)], prod[:, hf, 0, :], u_ready)
                            if smalls[hf] in (0, 1, 2):
                                ada_low()

                    def two_up(i):
                        if with_ada:
                            ada_low()
                        for e in range(2):
                            split((q0 + e) % 2)
                            up(i * 2 + 1 + e, SMALLS[e] if with_ada else NONE)
                    up(0, NONE)
                    loops.repeat(HK // 2, two_up, unit=2, pair0=2, pair1=2, ada=4 * with_ada, u=4, steps=4)
                    split(q0)
                    if with_ada:
                        coefficients(half + 1, layer)

                    def down(n, e, more=True):
                        update_x(n, e, s)
                        if more:
                            split((q0 + 1 + e) % 2)
                    end = half == 1 and last_stage
                    loops.repeat(KD // 2 - end, lambda i: [down(i * 2 + e, e) for e in range(2)], unit=2,
                                 pair0=1, pair1=1)
                    if end:
                        for e in range(2):
                            down(KD - 2 + e, e, more=False)

            def window_means(g, b):
                w = WINDOWS[g]
                sums_t.step(g + 1)
                dve.wait_ge(doubled, sums_t.at())
                src, other = win[g % 2], win[(g + 1) % 2]
                step(dve.tensor_tensor(first[:, :], src[:, HALO:HALO + 16],
                                       const[:, K_INV + 16 * g:K_INV + 16 * g + 16], ALU.mult))
                for a, n, c in ((HALO, TP, 0), (S0, TS, TP)):
                    step(dve.scalar_tensor_tensor(other[:, c:c + n], src[:, a:a + n], 1.0 / w, pf[:, b, a:a + n],
                                                  ALU.mult, ALU.subtract))
                settled()
                step(dve.tensor_tensor(other[:, 0:16], first[:, :], pf[:, b, HALO:HALO + 16], ALU.subtract))
                settled()
                two_parts(yp_hi[:, g, :], yp_lo[:, g, :], other[:, 0:T], yp_ready)

            def head(hd, layer):
                for b in range(JB):
                    sc_t.step()
                    dve.wait_ge(sc_ready, sc_t.at())
                    n = TP - b * P
                    dve.tensor_tensor(masked[:, b % 2, 0:n], const[:, K_MASK + hd * TP:K_MASK + hd * TP + n],
                                      (ps_mod, ps_misc)[b % 2][:, 0:n], ALU.mult).then_inc(masked_ok, 1)
                sc_t.step()
                dve.wait_ge(sc_ready, sc_t.at())
                dve.tensor_tensor(masked_s[0:TS, :], const[0:TS, K_MASK + hd * TP:K_MASK + hd * TP + TS],
                                  ps_sum[0:TS, 1, 0:TS], ALU.mult).then_inc(masked_ok, 1)
                dve.tensor_tensor(q_xi[:, :], q[:, hd, TP:T], const[:, K_XI + hd * TS:K_XI + (hd + 1) * TS],
                                  ALU.mult).then_inc(masked_ok, 1)
                pair0.step()
                dve.wait_ge(acc_ready[1], pair1.at(1))
                pair1.step()
                dve.wait_ge(s_out[hd % 2], layer * 64 + (32 * (hd // 2) + 32))
                dve.scalar_tensor_tensor(s_new[hd % 2][:, 1, :], s_old[:, hd, :], const[:, K_GBLK + hd:K_GBLK + hd + 1],
                                         acc[:, 3, 0:DK], ALU.mult, ALU.add)
                dve.tensor_copy(s_new[hd % 2][:, 0, :], acc[:, 2, 0:DK]).then_inc(acc_free[1], 1)

            def middle(layer):
                for kind, n in MID:
                    if kind == "w":
                        split(n)
                    if kind == "qk":
                        for hf in range(2):
                            swap_t.step()
                            dve.wait_ge(swapped, swap_t.at())
                            z = tmp[:, hf, :].rearrange("p (a t) -> p a t", a=2)
                            for a, (dst, scale) in enumerate(((q, 1.0), (k, DK ** -0.5))):
                                step(dve.scalar_tensor_tensor(dst[:, n, cols(hf)], acc[:, 2 * hf + a, 0:HT], scale,
                                                              cos[:, cols(hf)], ALU.mult, ALU.mult))
                                step(dve.scalar_tensor_tensor(z[:, a], z[:, a], scale, sin[:, cols(hf)],
                                                              ALU.mult, ALU.mult))
                            settled()
                            for a, dst in enumerate((q, k)):
                                last = dve.tensor_tensor(dst[:, n, cols(hf)], dst[:, n, cols(hf)], z[:, a], ALU.add)
                            last.then_inc(acc_free[hf], 1)
                            pairs[hf].step()
                    elif kind == "v":
                        for t in range(TOK):
                            pairs[(n * TOK + t) % 2].step()
                    elif kind == "pool":
                        if n:
                            tails.step()
                            dve.wait_ge(tails_t, tails.at())
                        step(dve.memset(pf[:, :, 0:HALO], 0.0))
                        cache = cache_t[:, :].rearrange("p (l t g) -> p l g t", l=DEPTH, g=GROUPS)
                        for b in range(2):
                            last = dve.tensor_copy(pf[:, b, HALO + TP:S0], cache[:, layer, 2 * n + b, :])
                        last.then_inc(halo_ready, 1)
                        for p in range(2):
                            pairs[p].step()
                    elif kind == "win":
                        window_means(n, n % 2)
                    elif kind == "map":
                        for e in range(2):
                            g = 2 * n + e
                            pairs[e].step()
                            freed(e)
                            two_parts(yp_hi[:, g, :], yp_lo[:, g, :], map_tile(g), side_ready)
                    elif kind == "head":
                        head(n, layer)
                    elif kind == "split":
                        y_t.step()
                        dve.wait_ge(y_copied, y_t.at(1))
                        two_parts(gn_hi[:, :], gn_lo[:, :], q[:, n, :], gn_split)
                    elif kind == "mean":
                        dve.wait_ge(acc_ready[0], pair0.at(1))
                        pair0.step()
                        y = halves(q[:, n, :])
                        dve.scalar_tensor_tensor(y, pair_banks(0), -1.0 / DK, y, ALU.mult, ALU.add)\
                            .then_inc(acc_free[0], 1)
                        sq_t.step()
                        dve.wait_ge(gn_squared, sq_t.at())
                        two_parts(gn_hi[:, :], gn_lo[:, :], tmp[:, 0, :], gn_split)
                    elif kind == "var":
                        pair0.step()
                    elif kind == "norm":
                        freed(0)
                        step(dve.reciprocal(rstd[:, :], rstd[:, :]))
                        settled()
                        step(dve.tensor_tensor(q[:, n, :], q[:, n, :], rstd[:, :], ALU.mult))
                    elif kind == "g":
                        for hf in range(2):
                            pairs[hf].step()
                    elif kind == "gate":
                        settled()
                        for hf in range(2):
                            freed(hf)
                            for b in range(2):
                                hd = 2 * n + b
                                last = dve.scalar_tensor_tensor(q[:, hd, cols(hf)], q[:, hd, cols(hf)],
                                                                vec_t[:, bass.ds(layer * R_ALL + (R_GN + hd), 1)],
                                                                acted[:, hf, b, :], ALU.mult, ALU.mult)
                            last.then_inc(gated, 1)
                            gated_t.step()
                    elif kind == "ret":
                        dve.wait_ge(gated, gated_t.at())
                        for hd in (2 * n, 2 * n + 1):
                            two_parts(ry_hi[:, hd, :], ry_lo[:, hd, :], q[:, hd, :], side_ready)
                for mh in range(2):
                    def gate_out(i):
                        for p in range(2):
                            pairs[p].step()
                        split(0)
                        for hf in range(2):
                            dve.wait_ge(acc_ready[hf], pairs[hf].at(1))
                            pairs[hf].step()
                            dve.scalar_tensor_tensor(prod[:, hf, :, :], acted[:, hf, :, :], 1.0, pair_banks(hf),
                                                     ALU.add, ALU.mult).then_inc(acc_free[hf], 1)
                            freed(hf)
                            step(dve.tensor_tensor(prod[:, hf, 0, :], prod[:, hf, 0, :], prod[:, hf, 1, :], ALU.add))
                            settled()
                            two_parts(m_hi[:, i, cols(hf)], m_lo[:, i, cols(hf)], prod[:, hf, 0, :], side_ready)
                        split(1)
                    loops.repeat(4, gate_out, unit=2, pair0=2, pair1=2, steps=4)

                    def outs(i):
                        for e in range(2):
                            for b in range(2):
                                n = i * 4 + (2 * e + b)
                                update_x(n, b, 1)
                            split(e)
                    loops.repeat(2, outs, unit=2, pair0=2, pair1=2)

            def one_layer(layer):
                split(0)
                split(1)
                reciprocal_root()
                split(2)
                split(3)
                loops.repeat(CHUNKS // 2 - 1, lambda i: [split(p) for p in range(4)], unit=4)
                split(0)
                split(1)
                coefficients(0, layer)
                ffn(layer, 0, True, False)
                reciprocal_root()
                make_h(1)
                middle(layer)
                reciprocal_root()
                ffn(layer, 2, False, True)
                tails.step()
                mask_t.step(24)
                gn_t.step(8)
                layers.step()
            loops.layers(one_layer)

            reciprocal_root()
            for kk in range(KD):
                dve.scalar_tensor_tensor(x[:, kk, :], x[:, kk, :], vec_t[:, R_FG + kk:R_FG + kk + 1], rstd[:, :],
                                         ALU.mult, ALU.mult).then_inc(h_ready[0], 1)


_INS = ["x_prompt", "x_sample", "c_prompt", "c_sample", "cache_pool", "state_ret", "w_ada", "b_ada", "norm_g",
        "w_up1", "w_down1", "w_up2", "w_down2", "w_in", "pool_map", "pool_scale", "w_pool_out", "ret_gn",
        "w_ret_out", "w_o", "final_g"]
_OUTS = [((1, TP, D), "float32"), ((1, TS, D), "float32"), ((DEPTH, 1, HALO, 512), "float32"),
         ((DEPTH, 1, HEADS, DK, DK), "float32"), ((DEPTH, 1, HALO, 512), "float32"),
         ((DEPTH, 1, HEADS, DK, DK), "float32")]


def constants():
    f32 = np.float32
    out = np.zeros((P, K_ALL), f32)
    out[:, K_ID:K_ID + P] = np.eye(P)
    out[:, K_ONE:K_ONE + P] = 1.0
    pos = np.concatenate([np.arange(TP), 1024 + np.arange(TS)]).astype(f32)
    inv = f32(10000.0) ** (-np.arange(64, dtype=f32) / f32(64))
    ang = (inv[:, None] * pos[None, :]).astype(f32).astype(np.float64)
    out[:, K_COS:K_COS + T] = np.tile(np.cos(ang), (2, 1))
    out[:, K_SIN:K_SIN + T] = np.concatenate([-np.sin(ang), np.sin(ang)])
    lg = np.log1p(-np.exp2(-5.0 - np.arange(HEADS)))
    p, c = np.arange(P)[:, None], np.arange(TP)[None, :]
    for h in range(HEADS):
        out[:, K_MASK + h * TP:K_MASK + (h + 1) * TP] = np.where(c >= p, np.exp(lg[h] * np.maximum(c - p, 0)), 0.0)
        out[:, K_XI + h * TS:K_XI + (h + 1) * TS] = np.exp(lg[h] * (np.arange(TS) + 1.0))
        for b in range(JB):
            out[:, K_ZETA + h * JB + b] = np.exp(lg[h] * (TP - 1.0 - b * P - np.arange(P)))
        out[:, K_ZETAS + h] = np.exp(lg[h] * np.maximum(TS - 1.0 - np.arange(P), 0))
        out[:, K_GBLK + h] = np.exp(lg[h] * TS)
    for g, w in enumerate(WINDOWS):
        out[:, K_INV + 16 * g:K_INV + 16 * (g + 1)] = 1.0 / np.minimum(w, np.arange(16) + 1.0)
    out[:, K_EPS] = EPS
    return out


def kernel(**inputs):
    import concourse.bacc as bacc
    from concourse.bass_utils import run_bass_kernel_spmd

    nc = bacc.Bacc("TRN2", target_bir_lowering=False, num_devices=1)
    arrays, args = {}, []
    for name in _INS:
        a = np.ascontiguousarray(inputs[name])
        arrays[f"in_{name}"] = a
        args.append(nc.dram_tensor(f"in_{name}", a.shape, mybir.dt.from_np(a.dtype), kind="ExternalInput").ap())
    arrays["in_consts"] = constants()
    args.append(nc.dram_tensor("in_consts", (P, K_ALL), F32, kind="ExternalInput").ap())
    for i, (shape, dtype) in enumerate(_OUTS):
        args.append(nc.dram_tensor(f"out_{i}", shape, mybir.dt.from_np(np.dtype(dtype)), kind="ExternalOutput").ap())
    trunk_kernel(nc, *args)
    r = run_bass_kernel_spmd(nc, [arrays], core_ids=[0])
    return tuple(r.results[0][f"out_{i}"] for i in range(len(_OUTS)))
```
